# Optimizing a Trainium2 kernel written in Bass

```python
import math
import jax, jax.numpy as jnp
from jax import lax
import numpy as np

D_MODEL = 1024
BATCH = 1
SEQ = 256
DEPTH = 2

CHUNK = 64
Q_BLOCK = 128
EPS = 1e-6
MASK_VALUE = -1e30
TINY = 1e-30
H_A = 4
DK_A = D_MODEL // 16
DV_A = 2 * DK_A
ROT_DIM = DK_A // 4
ROPE_THETA = 500000.0
H_B = 4
DK_B = D_MODEL // 16
DV_B = D_MODEL // 16
C_WIDTH = D_MODEL // 4
CONV_WIDTH = 3
D_MIX = H_A * DV_A + H_B * DV_B + C_WIDTH
SPLIT_SIZES = (H_A * 2 * DK_A, H_A * 2 * DK_A, H_A * DV_A,
               H_B * DK_B, H_B * DK_B, H_B * DV_B, H_B * DV_B,
               C_WIDTH, C_WIDTH, C_WIDTH)
D_IN = H_A * (4 * DK_A + DV_A) + H_B * (2 * DK_B + 2 * DV_B) + 3 * C_WIDTH
N_GROUPS = 4
EXPERTS_PER_GROUP = 8
N_EXPERTS = N_GROUPS * EXPERTS_PER_GROUP
TOP_K_INNER = 2
D_EXPERT = D_MODEL // 2
MOE_BLOCK = 256

kernel_name = "hymba_style_hybrid_diffattn_hgrn2_shortconv_hmoe"

def rms_norm(x, g):
    xf = x.astype(jnp.float32)
    y = xf * lax.rsqrt(jnp.mean(xf * xf, axis=-1, keepdims=True) + EPS)
    return (y * g.astype(jnp.float32)).astype(x.dtype)

def partial_rope(t, cos, sin):
    half = ROT_DIM // 2
    tf = t.astype(jnp.float32)
    t1, t2, rest = tf[..., :half], tf[..., half:ROT_DIM], tf[..., ROT_DIM:]
    out = jnp.concatenate([t1 * cos - t2 * sin, t1 * sin + t2 * cos, rest], axis=-1)
    return out.astype(t.dtype)

def differential_attention(q_in, k_in, v_in, positions, q_g, k_g, lq1, lk1, lq2, lk2, subln_g, layer_idx):
    b, s = q_in.shape[0], q_in.shape[1]
    q = rms_norm(q_in.reshape(b, s, H_A, 2, DK_A), q_g)
    k = rms_norm(k_in.reshape(b, s, H_A, 2, DK_A), k_g)
    v = v_in.reshape(b, s, H_A, DV_A)
    inv_freq = ROPE_THETA ** (-jnp.arange(0, ROT_DIM, 2, dtype=jnp.float32) / ROT_DIM)
    ang = positions.astype(jnp.float32)[..., None] * inv_freq
    cos = jnp.cos(ang)[:, :, None, None, :]
    sin = jnp.sin(ang)[:, :, None, None, :]
    q = partial_rope(q, cos, sin)
    k = partial_rope(k, cos, sin)
    lam_init = 0.8 - 0.6 * math.exp(-0.3 * layer_idx)
    lam = (jnp.exp(jnp.sum(lq1.astype(jnp.float32) * lk1.astype(jnp.float32)))
           - jnp.exp(jnp.sum(lq2.astype(jnp.float32) * lk2.astype(jnp.float32))) + lam_init)
    scale = DK_A ** -0.5
    pos_chunk = jnp.arange(s) // CHUNK
    outs = []
    for blk in range(s // Q_BLOCK):
        q_lo, q_hi = blk * Q_BLOCK, (blk + 1) * Q_BLOCK
        scores = jnp.einsum('bqhcd,bkhcd->bhcqk', q[:, q_lo:q_hi], k[:, :q_hi]).astype(jnp.float32) * scale
        mask = pos_chunk[None, :q_hi] <= pos_chunk[q_lo:q_hi, None]
        probs = jax.nn.softmax(jnp.where(mask, scores, MASK_VALUE), axis=-1)
        weights = probs[:, :, 0] - lam * probs[:, :, 1]
        outs.append(jnp.einsum('bhqk,bkhv->bqhv', weights.astype(v.dtype), v[:, :q_hi]))
    o = jnp.concatenate(outs, axis=1)
    o = rms_norm(o, subln_g) * (1.0 - lam_init)
    return o.reshape(b, s, H_A * DV_A)

def hgrn2(q_in, f_in, i_in, g_in, lb, norm_g):
    b, s = q_in.shape[0], q_in.shape[1]
    nc = s // CHUNK
    zf = f_in.reshape(b, s, H_B, DK_B).astype(jnp.float32)
    lbh = lb.reshape(H_B, DK_B).astype(jnp.float32)
    f = lbh + (1.0 - lbh) * jax.nn.sigmoid(zf)
    log_f = jnp.log(jnp.maximum(f, TINY))
    key = (1.0 - lbh) * jax.nn.sigmoid(-zf)
    q = jax.nn.silu(q_in.reshape(b, s, H_B, DK_B).astype(jnp.float32))
    v = i_in.reshape(b, s, H_B, DV_B).astype(jnp.float32)

    def to_chunks(t):
        return t.reshape(b, nc, CHUNK, H_B, t.shape[-1]).transpose(1, 0, 3, 2, 4)

    tri = (jnp.arange(CHUNK)[:, None] >= jnp.arange(CHUNK)[None, :])[:, :, None]

    def step(state, inp):
        qc, kc, vc, lfc = inp
        g = jnp.cumsum(lfc, axis=2)
        diff = g[:, :, :, None, :] - g[:, :, None, :, :]
        decay = jnp.where(tri, jnp.exp(jnp.where(tri, diff, 0.0)), 0.0)
        scores = jnp.einsum('bhtd,bhsd,bhtsd->bhts', qc, kc, decay)
        o = (jnp.einsum('bhts,bhsv->bhtv', scores, vc)
             + jnp.einsum('bhtd,bhdv->bhtv', qc * jnp.exp(g), state))
        g_last = g[:, :, -1:, :]
        new_state = (jnp.exp(g_last[:, :, 0, :])[..., None] * state
                     + jnp.einsum('bhsd,bhsv->bhdv', kc * jnp.exp(g_last - g), vc))
        return new_state, o

    state0 = jnp.zeros((b, H_B, DK_B, DV_B), jnp.float32)
    _, o = lax.scan(step, state0, (to_chunks(q), to_chunks(key), to_chunks(v), to_chunks(log_f)))
    o = o.transpose(1, 0, 3, 2, 4).reshape(b, s, H_B, DV_B)
    o = rms_norm(o, norm_g).reshape(b, s, H_B * DV_B) * jax.nn.silu(g_in.astype(jnp.float32))
    return o.astype(g_in.dtype)

def short_conv(b_gate, c_gate, x_in, conv_w):
    h = c_gate * x_in
    s = h.shape[1]
    hp = jnp.pad(h, ((0, 0), (CONV_WIDTH - 1, 0), (0, 0)))
    y = conv_w[0] * hp[:, 0:s]
    for j in range(1, CONV_WIDTH):
        y = y + conv_w[j] * hp[:, j:j + s]
    return b_gate * y

def hier_moe(h, wg, bg, we, be, w_gate, w_up, w_down):
    t, d = h.shape
    hf = h.astype(jnp.float32)
    g_logits = hf @ wg.astype(jnp.float32) + bg.astype(jnp.float32)
    p_group = jax.nn.softmax(g_logits, axis=-1)
    g_idx = jnp.argmax(g_logits, axis=-1)
    p_g = jnp.take_along_axis(p_group, g_idx[:, None], axis=-1)
    e_logits = (hf @ we.astype(jnp.float32) + be.astype(jnp.float32)).reshape(t, N_GROUPS, EXPERTS_PER_GROUP)
    e_in_group = jnp.take_along_axis(e_logits, g_idx[:, None, None], axis=1)[:, 0]
    top_val, top_idx = lax.top_k(e_in_group, TOP_K_INNER)
    gates = p_g * jax.nn.softmax(top_val, axis=-1)
    expert_id = (g_idx[:, None] * EXPERTS_PER_GROUP + top_idx).reshape(-1)
    token_id = jnp.repeat(jnp.arange(t), TOP_K_INNER)
    n_assign = t * TOP_K_INNER
    order = jnp.argsort(expert_id)
    sorted_e = expert_id[order]
    counts = jnp.bincount(expert_id, length=N_EXPERTS)
    padded = (counts + MOE_BLOCK - 1) // MOE_BLOCK * MOE_BLOCK
    pad_end = jnp.cumsum(padded)
    pad_start = pad_end - padded
    raw_start = jnp.cumsum(counts) - counts
    dest = pad_start[sorted_e] + jnp.arange(n_assign) - raw_start[sorted_e]
    cap = -(-n_assign // MOE_BLOCK) * MOE_BLOCK + N_EXPERTS * MOE_BLOCK
    n_blocks = cap // MOE_BLOCK
    buf = jnp.zeros((cap, d), h.dtype).at[dest].set(h[token_id[order]])
    blk_e = jnp.minimum(jnp.searchsorted(pad_end, jnp.arange(n_blocks) * MOE_BLOCK, side='right'), N_EXPERTS - 1)

    def expert_block(args):
        xb, e = args
        return (jax.nn.silu(xb @ w_gate[e]) * (xb @ w_up[e])) @ w_down[e]

    y_buf = lax.map(expert_block, (buf.reshape(n_blocks, MOE_BLOCK, d), blk_e)).reshape(cap, d)
    y_assign = jnp.zeros((n_assign, d), y_buf.dtype).at[order].set(y_buf[dest])
    return jnp.einsum('tk,tkd->td', gates.astype(y_assign.dtype), y_assign.reshape(t, TOP_K_INNER, d))

def setup_inputs(seed: int = 0) -> dict:
    key = jax.random.key(seed)
    ks = jax.random.split(key, 24)
    f32 = jnp.float32

    def nrm(k, shape, scale):
        return jax.random.normal(k, shape, f32) * scale

    def gain(k, shape):
        return 1.0 + 0.02 * jax.random.normal(k, shape, f32)

    x = jax.random.normal(ks[0], (BATCH, SEQ, D_MODEL), f32)
    offsets = jax.random.randint(ks[1], (BATCH, 1), 0, 64, dtype=jnp.int32) * CHUNK
    positions = (offsets + jnp.arange(SEQ, dtype=jnp.int32)[None, :]).astype(jnp.int32)
    return {
        "x": x,
        "positions": positions,
        "norm_mix_g": gain(ks[2], (DEPTH, D_MODEL)),
        "w_in": nrm(ks[3], (DEPTH, D_MODEL, D_IN), D_MODEL ** -0.5),
        "attn_q_norm_g": gain(ks[4], (DEPTH, DK_A)),
        "attn_k_norm_g": gain(ks[5], (DEPTH, DK_A)),
        "lambda_q1": nrm(ks[6], (DEPTH, DK_A), 0.1),
        "lambda_k1": nrm(ks[7], (DEPTH, DK_A), 0.1),
        "lambda_q2": nrm(ks[8], (DEPTH, DK_A), 0.1),
        "lambda_k2": nrm(ks[9], (DEPTH, DK_A), 0.1),
        "attn_subln_g": gain(ks[10], (DEPTH, DV_A)),
        "hgrn_lower_bounds": nrm(ks[11], (DEPTH, H_B * DK_B), 0.5),
        "hgrn_norm_g": gain(ks[12], (DEPTH, DV_B)),
        "conv_w": nrm(ks[13], (DEPTH, CONV_WIDTH, C_WIDTH), CONV_WIDTH ** -0.5),
        "w_out": nrm(ks[14], (DEPTH, D_MIX, D_MODEL), D_MIX ** -0.5),
        "norm_ffn_g": gain(ks[15], (DEPTH, D_MODEL)),
        "router_group_w": nrm(ks[16], (DEPTH, D_MODEL, N_GROUPS), D_MODEL ** -0.5),
        "router_group_b": nrm(ks[17], (DEPTH, N_GROUPS), 0.01),
        "router_expert_w": nrm(ks[18], (DEPTH, D_MODEL, N_EXPERTS), D_MODEL ** -0.5),
        "router_expert_b": nrm(ks[19], (DEPTH, N_EXPERTS), 0.01),
        "expert_w_gate": nrm(ks[20], (DEPTH, N_EXPERTS, D_MODEL, D_EXPERT), D_MODEL ** -0.5),
        "expert_w_up": nrm(ks[21], (DEPTH, N_EXPERTS, D_MODEL, D_EXPERT), D_MODEL ** -0.5),
        "expert_w_down": nrm(ks[22], (DEPTH, N_EXPERTS, D_EXPERT, D_MODEL), D_EXPERT ** -0.5),
    }

def reference(x, positions, norm_mix_g, w_in, attn_q_norm_g, attn_k_norm_g, lambda_q1, lambda_k1,
              lambda_q2, lambda_k2, attn_subln_g, hgrn_lower_bounds, hgrn_norm_g, conv_w, w_out,
              norm_ffn_g, router_group_w, router_group_b, router_expert_w, router_expert_b,
              expert_w_gate, expert_w_up, expert_w_down):
    b, s, d = x.shape
    lb_probs = jax.nn.softmax(hgrn_lower_bounds.astype(jnp.float32), axis=0)
    lower_bounds = jnp.cumsum(lb_probs, axis=0) - lb_probs[0:1]
    split_points = [int(v) for v in np.cumsum(SPLIT_SIZES)[:-1]]
    for l in range(DEPTH):
        u = rms_norm(x, norm_mix_g[l]) @ w_in[l]
        aq, ak, av, bq, bf, bi, bg, cb, cc, cx = jnp.split(u, split_points, axis=-1)
        o_a = differential_attention(aq, ak, av, positions, attn_q_norm_g[l], attn_k_norm_g[l],
                                     lambda_q1[l], lambda_k1[l], lambda_q2[l], lambda_k2[l],
                                     attn_subln_g[l], l)
        o_b = hgrn2(bq, bf, bi, bg, lower_bounds[l], hgrn_norm_g[l])
        o_c = short_conv(cb, cc, cx, conv_w[l])
        mix = jnp.concatenate([o_a.astype(x.dtype), o_b.astype(x.dtype), o_c.astype(x.dtype)], axis=-1)
        x = x + mix @ w_out[l]
        h = rms_norm(x, norm_ffn_g[l]).reshape(b * s, d)
        y = hier_moe(h, router_group_w[l], router_group_b[l], router_expert_w[l], router_expert_b[l],
                     expert_w_gate[l], expert_w_up[l], expert_w_down[l])
        x = x + y.reshape(b, s, d).astype(x.dtype)
    return x


_drawn_inputs = setup_inputs


def setup_inputs(seed=0):
    import zlib

    import numpy as np

    out = dict(_drawn_inputs(seed))
    spreads = {}
    factors = {'attn_k_norm_g': 2.931,
     'hgrn_lower_bounds': 2.819,
     'hgrn_norm_g': 4.457,
     'router_group_b': 14.993,
     'router_expert_b': 10.726,
     'lambda_q2': 3.245,
     'attn_subln_g': 3.07,
     'norm_ffn_g': 3.719}
    for name, (base, spread) in spreads.items():
        noise = np.random.default_rng([zlib.crc32(name.encode()), seed]).standard_normal(out[name].shape)
        drawn = base * np.exp(spread * noise) if base else spread * noise
        out[name] = __import__('jax').numpy.asarray(drawn.astype(out[name].dtype))
    for name, factor in factors.items():
        out[name] = (out[name] * factor).astype(out[name].dtype)
    return out
```

```python
import math
from contextlib import ExitStack

import numpy as np
import concourse.bass as bass
from concourse import mybir

F32 = mybir.dt.float32
I32 = mybir.dt.int32
U32 = mybir.dt.uint32
ALU = mybir.AluOpType
ACT = mybir.ActivationFunctionType
AX = mybir.AxisListType.X
ds = bass.ds

P = 128


CONSTS = 47
DVE_M = 232
DVE_G = 21
POOL_M = 2


class Signal:

    def __init__(self, sem, per, credit=0):
        self.sem, self.per, self.credit = sem, per, credit

    def after(self, turn, n):
        return turn * self.per + (n + self.credit)


class Chain:

    def __init__(self, signal, turn):
        self.own, self.turn, self.sem, self.n = signal, turn, signal.sem, 0

    def step(self):
        self.n += 1
        return self.sem

    def last(self):
        return self.own.after(self.turn, self.n)

    def end(self):
        assert self.n == self.own.per, (self.sem, self.n, self.own.per)


def hybrid_trunk(nc, a, out):
    DEPTH, D = a["norm_mix_g"].shape
    SEQ = a["x"].shape[1]
    D_IN = a["w_in"].shape[2]
    TI = SEQ // P
    KT = D // P
    DK = a["attn_q_norm_g"].shape[1]
    DV = a["attn_subln_g"].shape[1]
    HA = 4
    HC = 2 * HA
    HALF = DK // 8
    DB = a["hgrn_norm_g"].shape[1]
    HB = 4
    HP = HB * DB // P
    CW = a["conv_w"].shape[2]
    NG = a["router_group_w"].shape[2]
    NE = a["router_expert_w"].shape[2]
    EPG = NE // NG
    DE = a["expert_w_gate"].shape[3]
    CHUNK = 64
    EPS, TINY, MASKED = 1e-6, 1e-30, -1e30
    NK = 2
    CAP = 32
    UG = 4
    GROUPS = NE // UG
    MAXX = SEQ * NK // CAP
    R = 6
    SLOT = 4096
    LN_CUT = 2.0 ** -60
    assert TI == 2 and KT == 8 and HP == 2 and CW == 2 * P and DE == 4 * P

    ctx = ExitStack()
    with ctx:
        def sb(name, shape, dt=F32):
            return ctx.enter_context(nc.sbuf_tensor(name, shape, dt))

        def sig(name, per, credit=0):
            return Signal(ctx.enter_context(nc.semaphore(name)), per, credit)

        ring = sb("ring", [P, R, SLOT])
        x = sb("x", [P, TI, D])
        h = sb("h", [P, TI, KT, P])
        hT = sb("hT", [P, KT, SEQ])
        mixT = hT
        ident = sb("ident", [P, P])
        before = sb("before", [P, P])
        ones = sb("ones", [P, P])
        iota = sb("iota", [P, P])
        LEVELS = [0, 64, 32, 16, 8, 4, 2, 1]
        masks = sb("masks", [P, len(LEVELS), P])
        restart = sb("restart", [P, HP, SEQ])
        attn_mask = sb("attn_mask", [P, CHUNK])
        cosb = sb("cosb", [P, TI, HALF])
        sinb = sb("sinb", [P, TI, HALF])
        table = sb("table", [P, DEPTH, 11])
        cur = sb("cur", [P, 11])
        prow = sb("prow", [DEPTH * 8, P])
        pcol = sb("pcol", [P, DEPTH * 8])
        pos_i = sb("pos_i", [P, TI], I32)
        small = sb("small", [P, 512])
        gmix = sb("gmix", [P, KT])
        gffn = sb("gffn", [P, KT])
        gffn_in = sb("gffn_in", [P, KT])
        wr = sb("wr", [P, KT, NG + NE])
        qkg = sb("qkg", [P, 2, DK])
        subg = sb("subg", [P, DV])
        hng = sb("hng", [P, DB])
        rb = sb("rb", [P, NG + NE])
        lamv = sb("lamv", [P, 4, DK])
        xinfo = sb("xinfo", [1, DEPTH, 2 + MAXX], I32)
        u = sb("u", [P, 13, 512])
        qkT = sb("qkT", [P, HC, SEQ])
        sm = sb("sm", [P, HC, SEQ])
        hg = sb("hg", [P, 6, 512])
        sT = sb("sT", [P, 2, HP * TI, P])
        far = sb("far", [P, 2, HP, P])

        G_, Q_, KEY_, D_, Z0_ = 0, 1, 2, 3, 4
        sq_junk = qkT[:, :, :].rearrange("p m n -> p (m n)")
        wT = hg[:, 0:3, :].rearrange("p a (n k) -> p (a n) k", k=P)
        bq, bf, aq, cbT, ccT, cxT = u[:, 0, :], u[:, 1, :], u[:, 2:6, :], u[:, 10, :], u[:, 11, :], u[:, 12, :]
        av = u[:, 6:8, :]
        bib = u[:, 8:10, :]
        qk = aq.rearrange("p (j i) n -> p j i n", j=2)
        att_w = u[:, 2:4, :].rearrange("p a n -> p (a n)").rearrange("p (h k) -> p h k", h=HA)
        oa = u[:, 4:6, :]
        ob = hg[:, Z0_, :]
        egate = hg[:, D_, :]
        xg = u[:, 0:4, :].rearrange("p a n -> p (a n)")[:, 0:KT * P].rearrange("p (k c) -> p k c", k=KT)
        ye = u[:, 4:6, :].rearrange("p a n -> p (a n)")
        sel = u[:, 6, 0:TI * P].rearrange("p (i c) -> p i c", i=TI)
        gat = u[:, 6, TI * P:2 * TI * P].rearrange("p (i c) -> p i c", i=TI)
        gtmp = u[:, 7, 0:TI * P].rearrange("p (i c) -> p i c", i=TI)
        gatT = u[:, 7, TI * P:2 * TI * P]
        sil = u[:, 8, 0:P]
        actv = u[:, 8, P:2 * P]
        actT = u[:, 8, 2 * P:3 * P]
        silr = u[:, 8, 3 * P:4 * P]
        smf = sm[:, :, :].rearrange("p m n -> p (m n)")
        rt, rt2, rt3 = u[:, 9, :], u[:, 10, :], u[:, 11, :]
        lg = rt[:, 0:TI * 40].rearrange("p (i n) -> p i n", i=TI)
        mg = rt[:, 80:96].rearrange("p (i n) -> p i n", i=TI)
        nmg, gidx, edif = rt[:, 96:98], rt[:, 98:100], rt[:, 196:198]
        ohg = rt[:, 100:108].rearrange("p (i n) -> p i n", i=TI)
        pen = rt[:, 108:116].rearrange("p (i n) -> p i n", i=TI)
        em = rt[:, 116:180].rearrange("p (i n) -> p i n", i=TI)
        mv = rt[:, 180:196].rearrange("p (i n) -> p i n", i=TI)
        eidf = rt[:, 198:202]
        eid = eidf.rearrange("p (k i) -> p k i", k=NK)
        rjunk = rt[:, 202:210].rearrange("p (i n) -> p i n", i=TI)
        picks = rt[:, 256:256 + TI * NE].rearrange("p (i n) -> p i n", i=TI)
        oh = rt[:, 320:320 + NK * TI * NE].rearrange("p (m n) -> p m n", n=NE)
        units, upto = rt[:, 448:448 + NE], rt[:, 480:480 + NE]
        prod4 = rt2[:, 0:NK * TI * NE].rearrange("p (m n) -> p m n", n=NE)
        over = rt2[:, 128:128 + NE * (SEQ // CAP - 1)].rearrange("p (n m) -> p n m", n=NE)
        base4, rank4, full4, fg4, xe = rt2[:, 384:388], rt2[:, 388:392], rt2[:, 392:396], rt2[0:1, 396:400], rt2[0:1, 400:416]
        ranks = rt2[:, 416:512]
        later = rt3[0:1, 0:MAXX * NE].rearrange("p (m n) -> p m n", n=NE)
        idx = sb("idx", [P, 2 * TI, 8], U32)

        def col(a0, n):
            return small[:, a0:a0 + n]

        ssq, lnv, rstd = col(0, 2), col(2, 2), col(4, 2)
        qk_ms, qk_rs = col(8, 16), col(24, 16)
        negmax, denom, inv = col(40, 16), col(56, 16), col(72, 16)
        oa_ms, oa_rs = col(88, 8), col(96, 8)
        ob_ms, ob_rs = col(104, 8), col(112, 8)
        lam_s, lam_e, nlam, subs = col(120, 2), col(122, 2), col(124, 1), col(125, 1)
        codes, gates = col(128, 4), col(132, 4)
        xsum = col(136, 1)
        fgrp = col(140, 4)
        thr_cap = col(144, SEQ // CAP - 1)
        thr_grp = col(152, MAXX // UG)
        pos_f, ang = col(160, 2), col(168, TI * HALF)
        turn_n, angc = col(184, TI * HALF), col(200, TI * HALF)
        freq = col(216, HALF)
        lbt = col(224, DEPTH * HP)
        lbm = col(232, HP)
        lbs = col(236, HP)
        eps = col(240, 1)
        expsum = col(248, 2)
        rs_v, rs_h, rs_w = col(256, 16), col(272, 16), col(288, 16)
        subgl = sb("subgl", [P, DV])

        bank = [ctx.enter_context(nc.psum_tensor(f"bank{i}", [P, 512], F32)) for i in range(8)]

        x_in, pos_in, rows_in, out_done = sig("x_in", 0), sig("pos_in", 0), sig("rows_in", 0), sig("out_done", 0)
        const_ok = sig("const_ok", CONSTS)
        settled = sig("settled", 0)
        dve_p = sig("dve_p", 0)
        pro_dve, pro_act, pro_pe = sig("pro_dve", 0), sig("pro_act", 0), sig("pro_pe", 0)
        params_in = sig("params_in", 16 * 14)
        ring_full = [sig(f"ring_full{i}", 16 * (18 if i < 3 else 17)) for i in range(R)]
        xring_full = [sig(f"xring_full{i}", 32) for i in range(R)]
        dve_m = sig("dve_m", DVE_M)
        sums_ok, h_ok, ht_ps, ht_sb = sig("sums_ok", 4), sig("h_ok", 4), sig("ht_ps", 8), sig("ht_sb", 8)
        proj_ps, proj_sb = sig("proj_ps", 13), sig("proj_sb", 13)
        hg_dve, hg_act, hg_qk = sig("hg_dve", 2), sig("hg_act", 3), sig("hg_qk", 1)
        z_diff, z_exp, z_ok = sig("z_diff", 8), sig("z_exp", 8), sig("z_ok", 8)
        lev_ps, lev_sb = sig("lev_ps", 9), sig("lev_sb", 9)
        qk_sq, qk_ok = sig("qk_sq", 2), sig("qk_ok", 2)
        qkt_ps, qkt_sb = sig("qkt_ps", 4), sig("qkt_sb", 4)
        sc_ps, max_ok, exp_ok, w_ok = sig("sc_ps", 2), sig("max_ok", 2), sig("exp_ok", 2), sig("w_ok", 2)
        wt_ps, wt_sb, pv_ps = sig("wt_ps", 3), sig("wt_sb", 3), sig("pv_ps", 2)
        oa_sq, oa_ok, oat_ps, oat_sb = sig("oa_sq", 2), sig("oa_ok", 2), sig("oat_ps", 2), sig("oat_sb", 2)
        gate_exp, ob_ps, ob_sq = sig("gate_exp", 1), sig("ob_ps", 1), sig("ob_sq", 1)
        ob_ok, obt_ps, obt_sb = sig("ob_ok", 1), sig("obt_ps", 1), sig("obt_sb", 1)
        pool_m = sig("pool_m", POOL_M)
        conv_in, taps_ok = sig("conv_in", 1), sig("taps_ok", 1)
        conv_ok, lam_sum, lam_exp = sig("conv_ok", 1), sig("lam_sum", 1), sig("lam_exp", 1)
        op_ps, x_mixed = sig("op_ps", 4), sig("x_mixed", 4)
        log_ps, top_g, exp_g = sig("log_ps", 1), sig("top_g", 1), sig("exp_g", 1)
        top_e, exp_e, picks_ok = sig("top_e", 1), sig("exp_e", 1), sig("picks_ok", 1)
        rank_ps, routed = sig("rank_ps", 1), sig("routed", 1)

        class Experts:

            def __init__(self, t, full):
                self.dve = sig(t + "dve", DVE_G, 1)
                self.sel_ok, self.gath_ps, self.xg_ok = sig(t + "sel_ok", 1), sig(t + "gath_ps", 2), sig(t + "xg_ok", 2)
                self.gat_ps, self.gat_sb = sig(t + "gat_ps", 1), sig(t + "gat_sb", 1)
                self.gu_ps, self.gu_exp, self.act_ok = sig(t + "gu_ps", 4, 2), sig(t + "gu_exp", 4), sig(t + "act_ok", 4)
                self.at_ps, self.at_sb = sig(t + "at_ps", 4), sig(t + "at_sb", 4)
                self.ye_ps, self.ye_act, self.ye_dve = sig(t + "ye_ps", 4, 2), sig(t + "ye_act", 4), sig(t + "ye_dve", 4)
                self.scat_ps, self.x_added = sig(t + "scat_ps", 4), sig(t + "x_added", 4, 1)
                self.full = full

        main = Experts("m_", ring_full)
        extra = Experts("x_", xring_full)

        block = ctx.enter_context(nc.Block())

        c_aq, c_ak, c_av, c_bq, c_bi, c_cb, c_cx = 0, 512, 1024, 1536, 2048, 2560, 3072
        assert c_cx + CW == D_IN
        SECTIONS = [(c_bq, 512, 3), (c_aq, 512, 4), (c_ak, 512, 5), (c_av, 512, 0), (c_bi, 512, 1), (c_cb, 512, 2),
                    (c_cx, 256, 0)]
        WOUT = (1, 2)

        def slots_of(i):
            return (3, 4, 5) if i % 2 == 0 else (0, 1, 2)

        def settle(e):
            e.sem_inc(settled.sem, 1)

        def extra_groups(e, l):
            e.wait_ge(routed.sem, routed.after(l, 1))
            settle(e)
            count = e.value_load(xinfo[0:1, ds(l, 1), 0:1], min_val=0, max_val=MAXX // UG)
            prior = e.value_load(xinfo[0:1, ds(l, 1), 1:2], min_val=0, max_val=DEPTH * MAXX // UG)
            return count, prior

        def layer_sums(e, l, count, prior):
            e.wait_ge(main.x_added.sem, main.x_added.after(l * GROUPS + GROUPS, 0))
            e.wait_ge(extra.x_added.sem, extra.x_added.after(prior + count, 0))

        def layer_parameters(e, l):
            def row(name):
                return a[name][ds(l, 1)].to_broadcast([P, a[name].shape[1]])

            for dst, src in (
                    (gmix[:, :], a["norm_mix_g"][ds(l, 1)].rearrange("l (p k) -> p (l k)", k=KT)),
                    (lamv[:, 0, :], row("lambda_q1")), (lamv[:, 1, :], row("lambda_k1")),
                    (lamv[:, 2, :], row("lambda_q2")), (lamv[:, 3, :], row("lambda_k2")),
                    (gffn_in[:, :], a["norm_ffn_g"][ds(l, 1)].rearrange("l (p k) -> p (l k)", k=KT)),
                    (qkg[:, 0, :], row("attn_q_norm_g")), (qkg[:, 1, :], row("attn_k_norm_g")),
                    (subg[:, :], row("attn_subln_g")), (hng[:, :], row("hgrn_norm_g")),
                    (rb[:, 0:NG], row("router_group_b")), (rb[:, NG:NG + NE], row("router_expert_b")),
                    (wr[:, :, 0:NG], a["router_group_w"][ds(l, 1)].rearrange("l (p k) n -> p (l k) n", k=KT)),
                    (wr[:, :, NG:NG + NE], a["router_expert_w"][ds(l, 1)].rearrange("l (p k) n -> p (l k) n", k=KT))):
                e.dma_start(dst, src).then_inc(params_in.sem, 16)

        @block.sync
        def _(e):
            e.dma_start(prow[0:DEPTH * HP, :], a["hgrn_lower_bounds"].rearrange("l (h p) -> (l h) p", p=P)).then_inc(rows_in.sem, 16)
            e.dma_start(prow[DEPTH * HP:DEPTH * 8, :], a["conv_w"].rearrange("l j (c p) -> (l j c) p", p=P)).then_inc(rows_in.sem, 16)
            e.dma_start(pos_i[:, :], a["positions"][0].rearrange("(i p) -> p i", p=P),
                        allow_slow_non_contiguous=True).then_inc(pos_in.sem, 16)
            e.dma_start(x[:, :, :], a["x"][0].rearrange("(i p) d -> p i d", p=P)).then_inc(x_in.sem, 16)
            layer_parameters(e, 0)
            with e.Fori(0, DEPTH) as l:
                w_in = a["w_in"][ds(l, 1)].rearrange("l (p k) n -> p (l k) n", k=KT)
                w_out = a["w_out"][ds(l, 1)].rearrange("l (k p) n -> p (l k) n", k=KT)

                def section(n):
                    c0, width, s = SECTIONS[n]
                    e.dma_start(ring[:, s, 0:KT * width].rearrange("p (k n) -> p k n", k=KT),
                                w_in[:, :, c0:c0 + width]).then_inc(ring_full[s].sem, 16)

                def unit(full, slots, ex, waits):
                    for n, (s, wait) in enumerate(zip(slots, waits)):
                        wait()
                        if n < 2:
                            src = a[("expert_w_gate", "expert_w_up")[n]][ds(l, 1), ds(ex, 1)].rearrange("l e (p k) n -> p (l e k n)", k=KT)
                            e.dma_start(ring[:, s, :], src).then_inc(full[s].sem, 16)
                        else:
                            src = a["expert_w_down"][ds(l, 1), ds(ex, 1)].rearrange("l e (j p) n -> p (l e j) n", p=P)
                            e.dma_start(ring[:, s, :].rearrange("p (j n) -> p j n", j=4), src).then_inc(full[s].sem, 16)

                def unit_waits(S, turn, i):
                    gu = lambda: e.wait_ge(S.gu_ps.sem, S.gu_ps.after(turn, i - 1))
                    return gu, gu, lambda: e.wait_ge(S.ye_ps.sem, S.ye_ps.after(turn, i - 1))

                first = l * GROUPS
                e.wait_ge(main.gu_ps.sem, main.gu_ps.after(first, -1))
                section(0)
                section(1)
                e.wait_ge(main.ye_ps.sem, main.ye_ps.after(first, -1))
                section(2)
                e.wait_ge(main.gu_ps.sem, main.gu_ps.after(first, 0))
                section(3)
                section(4)
                e.wait_ge(main.ye_ps.sem, main.ye_ps.after(first, 0))
                section(5)
                unit(ring_full, slots_of(0), 0,
                     [lambda n=n: e.wait_ge(proj_ps.sem, proj_ps.after(l, n)) for n in (2, 4, 6)])
                e.wait_ge(proj_ps.sem, proj_ps.after(l, 8))
                section(6)
                for n in range(2):
                    e.wait_ge(proj_ps.sem, proj_ps.after(l, 10 + 2 * n))
                    e.dma_start(ring[:, WOUT[n], :].rearrange("p (k n) -> p k n", k=KT),
                                w_out[:, :, n * 512:n * 512 + 512]).then_inc(ring_full[WOUT[n]].sem, 16)
                op = lambda: e.wait_ge(op_ps.sem, op_ps.after(l, 4))
                unit(ring_full, slots_of(1), 1, [lambda: e.wait_ge(proj_ps.sem, proj_ps.after(l, 13)), op, op])
                for i in range(2, UG):
                    unit(ring_full, slots_of(i), i, unit_waits(main, first, i))
                with e.Fori(1, GROUPS) as g:
                    for i in range(UG):
                        unit(ring_full, slots_of(i), g * UG + i, unit_waits(main, l * GROUPS + g, i))
                count, prior = extra_groups(e, l)
                with e.If(count > 0):
                    with e.Fori(0, count) as t:
                        e.wait_ge(main.x_added.sem, main.x_added.after(l * GROUPS + GROUPS, 0))
                        for i in range(UG):
                            ex = e.value_load(xinfo[0:1, ds(l, 1), ds(t * UG + (2 + i), 1)], min_val=0, max_val=NE - 1)
                            unit(xring_full, slots_of(i), ex, unit_waits(extra, prior + t, i))
                        e.wait_ge(extra.x_added.sem, extra.x_added.after(prior + t, 4))
                        settle(e)
            count, prior = extra_groups(e, DEPTH - 1)
            layer_sums(e, DEPTH - 1, count, prior)
            e.dma_start(out[0].rearrange("(i p) d -> p i d", p=P), x[:, :, :]).then_inc(out_done.sem, 16)
            e.wait_ge(out_done.sem, 16)

        @block.gpsimd
        def _(e):
            def short_convolution(e, l):
                c = Chain(pool_m, l)
                G = nc.gpsimd
                e.wait_ge(proj_sb.sem, proj_sb.after(l, 13))
                G.tensor_tensor(ccT, ccT, cxT, ALU.mult).then_inc(conv_in.sem, 1)
                e.wait_ge(taps_ok.sem, taps_ok.after(l, 1))
                for back, tap in ((1, bq), (2, bf)):
                    y, t = (v.rearrange("p (c t) -> p c t", c=2) for v in (cxT, tap))
                    G.tensor_tensor(y[:, :, back:SEQ], y[:, :, back:SEQ], t[:, :, 0:SEQ - back], ALU.add).then_inc(c.step(), 1)
                    e.wait_ge(c.sem, c.last())
                G.tensor_tensor(mixT[:, 6:8, :], cxT.rearrange("p (c t) -> p c t", c=2),
                                cbT.rearrange("p (c t) -> p c t", c=2), ALU.mult).then_inc(conv_ok.sem, 1)
                c.end()

            made = Chain(const_ok, 0)

            nc.gpsimd.memset(ident[:, :], 0.0).then_inc(made.step(), 1)
            nc.gpsimd.memset(before[:, :], 1.0).then_inc(made.step(), 1)
            nc.gpsimd.memset(ones[:, :], 1.0).then_inc(made.step(), 1)
            nc.gpsimd.memset(eps, EPS).then_inc(made.step(), 1)
            inv_freq = np.float32(500000.0) ** (-np.arange(0, 2 * HALF, 2, dtype=np.float32) / np.float32(2 * HALF))
            for n in range(HALF):
                nc.gpsimd.memset(freq[:, n:n + 1], float(inv_freq[n])).then_inc(made.step(), 1)
            e.wait_ge(made.sem, made.last())
            nc.gpsimd.affine_select(out=ident[:, :], in_=ident[:, :], compare_op=ALU.not_equal, fill=1.0,
                                    base=0, pattern=[[-1, P]], channel_multiplier=1).then_inc(made.step(), 1)
            nc.gpsimd.affine_select(out=before[:, :], in_=before[:, :], compare_op=ALU.is_gt, fill=0.0,
                                    base=0, pattern=[[1, P]], channel_multiplier=-1).then_inc(made.step(), 1)
            nc.gpsimd.iota(iota[:, :], [[1, P]], base=0, channel_multiplier=0, allow_small_or_imprecise_dtypes=True).then_inc(made.step(), 1)
            nc.gpsimd.iota(thr_cap, [[CAP, SEQ // CAP - 1]], base=CAP, channel_multiplier=0, allow_small_or_imprecise_dtypes=True).then_inc(made.step(), 1)
            nc.gpsimd.iota(thr_grp, [[UG, MAXX // UG]], base=0, channel_multiplier=0, allow_small_or_imprecise_dtypes=True).then_inc(made.step(), 1)
            nc.gpsimd.memset(xsum, 0.0).then_inc(made.step(), 1)
            for n in range(DEPTH):
                nc.gpsimd.memset(table[:, n, 10:11], 0.8 - 0.6 * math.exp(-0.3 * n)).then_inc(made.step(), 1)
            nc.gpsimd.memset(restart[:, :, :], 1.0).then_inc(made.step(), 1)
            nc.gpsimd.memset(masks[:, :, :], 0.0).then_inc(made.step(), 1)
            nc.gpsimd.memset(attn_mask[:, :], MASKED).then_inc(made.step(), 1)
            e.wait_ge(made.sem, made.last())
            nc.gpsimd.affine_select(out=attn_mask[:, :], in_=attn_mask[:, :], compare_op=ALU.is_ge, fill=0.0,
                                    base=CHUNK - 1, pattern=[[0, CHUNK]], channel_multiplier=-1).then_inc(made.step(), 1)
            nc.gpsimd.memset(restart[:, :, :].rearrange("p h (c t) -> p (h c) t", t=CHUNK)[:, :, 0:1], 0.0).then_inc(made.step(), 1)
            nc.gpsimd.affine_select(out=masks[:, 0, :], in_=masks[:, 0, :], compare_op=ALU.not_equal, fill=1.0,
                                    base=0, pattern=[[-1, P]], channel_multiplier=1).then_inc(made.step(), 1)

            def second_blocks(n, B):
                return masks[:, n, :].rearrange("p (b o t) -> p b o t", o=2, t=B)[:, :, 1, :]

            for n, B in enumerate(LEVELS[1:], 1):
                nc.gpsimd.memset(second_blocks(n, B), 1.0).then_inc(made.step(), 1)
            e.wait_ge(made.sem, made.last())
            for n, B in enumerate(LEVELS[1:], 1):
                v = second_blocks(n, B)
                nc.gpsimd.affine_select(out=v, in_=v, compare_op=ALU.is_ge, fill=0.0, base=0,
                                        pattern=[[-2 * B, P // (2 * B)], [0, B]], channel_multiplier=1).then_inc(made.step(), 1)
            e.wait_ge(made.sem, made.last())
            for n, B in enumerate(LEVELS[1:], 1):
                v = second_blocks(n, B)
                nc.gpsimd.affine_select(out=v, in_=v, compare_op=ALU.is_ge, fill=0.0, base=B - 1,
                                        pattern=[[2 * B, P // (2 * B)], [0, B]], channel_multiplier=-1).then_inc(made.step(), 1)
            made.end()
            with e.Fori(0, DEPTH) as l:
                short_convolution(e, l)

        @block.tensor
        def _(e):
            T = nc.tensor
            for S in (main, extra):
                e.sem_inc(S.gu_ps.sem, 2)
                e.sem_inc(S.ye_ps.sem, 2)
            e.wait_ge(const_ok.sem, CONSTS)
            e.wait_ge(rows_in.sem, 32)
            T.transpose(bank[0][:, 0:DEPTH * 8], prow[:, :], ident[0:DEPTH * 8, 0:DEPTH * 8]).then_inc(pro_pe.sem, 1)
            e.wait_ge(pro_dve.sem, 1)

            def transposed_rows(l, which):
                for i in range(TI):
                    e.wait_ge(h_ok.sem, h_ok.after(l, 2 * which + i + 1))
                    for half in range(2):
                        for k in range(4):
                            last = T.transpose(bank[2 * i + half][:, k * P:k * P + P], h[:, i, 4 * half + k, :], ident[:, :])
                        last.then_inc(ht_ps.sem, 1)

            def experts(S, turn, loaded):
                e.wait_ge(S.sel_ok.sem, S.sel_ok.after(turn, 1))
                for half in range(2):
                    for k in range(4):
                        for i in range(TI):
                            last = T.matmul(bank[half][:, k * P:k * P + P], h[:, i, 4 * half + k, :], sel[:, i, :],
                                            start=(i == 0), stop=(i == TI - 1))
                    last.then_inc(S.gath_ps.sem, 1)
                for i in range(TI):
                    last = T.transpose(bank[2][:, i * P:i * P + P], gat[:, i, :], ident[:, :])
                last.then_inc(S.gat_ps.sem, 1)
                e.wait_ge(S.xg_ok.sem, S.xg_ok.after(turn, 2))
                for i in range(UG):
                    sg, su, sd = slots_of(i)
                    e.wait_ge(S.full[sg].sem, loaded(sg, i))
                    e.wait_ge(S.full[su].sem, loaded(su, i))
                    gate_up = ring[:, sg:su + 1, :].rearrange("p a (k n) -> p a k n", k=KT)
                    for k in range(KT):
                        for j in range(4):
                            last = T.matmul(bank[4][CAP * j:CAP * j + CAP, 0:2 * P], xg[:, k, CAP * i:CAP * i + CAP],
                                            gate_up[:, :, k, P * j:P * j + P], start=(k == 0), stop=(k == KT - 1))
                    last.then_inc(S.gu_ps.sem, 1)
                    e.wait_ge(S.act_ok.sem, S.act_ok.after(turn, i + 1))
                    T.transpose(bank[3][:, 0:P], actv, ident[:, :]).then_inc(S.at_ps.sem, 1)
                    if i:
                        e.wait_ge(S.ye_act.sem, S.ye_act.after(turn, i))
                        e.wait_ge(S.ye_dve.sem, S.ye_dve.after(turn, i))
                    e.wait_ge(S.full[sd].sem, loaded(sd, i))
                    e.wait_ge(S.at_sb.sem, S.at_sb.after(turn, i + 1))
                    down = ring[:, sd, :].rearrange("p (j n) -> p j n", j=4)
                    for j in range(4):
                        for q in range(4):
                            last = T.matmul(bank[5][CAP * q:CAP * q + CAP, 0:2 * P], actT[:, CAP * j:CAP * j + CAP],
                                            down[:, j, 2 * P * q:2 * P * q + 2 * P], start=(j == 0), stop=(j == 3))
                    last.then_inc(S.ye_ps.sem, 1)
                e.wait_ge(S.gat_sb.sem, S.gat_sb.after(turn, 1))
                e.wait_ge(S.ye_act.sem, S.ye_act.after(turn, 4))
                e.wait_ge(S.ye_dve.sem, S.ye_dve.after(turn, 4))
                for n in range(4):
                    i, half = n // 2, n % 2
                    if n >= 2:
                        e.wait_ge(S.x_added.sem, S.x_added.after(turn, n - 1))
                    T.matmul(bank[6 + n % 2][:, :], gatT[:, i * P:i * P + P], ye[:, half * 512:half * 512 + 512],
                             start=True, stop=True).then_inc(S.scat_ps.sem, 1)

            with e.Fori(0, DEPTH) as l:
                transposed_rows(l, 0)

                def section(n):
                    c0, width, s = SECTIONS[n]
                    e.wait_ge(ring_full[s].sem, ring_full[s].after(l, 32 if n == 6 else 16))
                    return ring[:, s, 0:KT * width].rearrange("p (k n) -> p k n", k=KT)

                def project_rows(W, b, i):
                    for k in range(KT):
                        last = T.matmul(bank[b][:, :], hT[:, k, i * P:i * P + P], W[:, k, :],
                                        start=(k == 0), stop=(k == KT - 1))
                    last.then_inc(proj_ps.sem, 1)

                def project_columns(W, b, pair):
                    for c in range(2):
                        for k in range(KT):
                            c0 = pair * 256 + c * P
                            last = T.matmul(bank[b][:, c * SEQ:c * SEQ + SEQ], W[:, k, c0:c0 + P], hT[:, k, :],
                                            start=(k == 0), stop=(k == KT - 1))
                    last.then_inc(proj_ps.sem, 1)

                def proj_read(n):
                    e.wait_ge(proj_sb.sem, proj_sb.after(l, n))

                def level(n):
                    if n == 0:
                        e.wait_ge(hg_qk.sem, hg_qk.after(l, 1))
                        left, right = hg[:, KEY_, :], hg[:, Q_, :]
                    else:
                        e.wait_ge(lev_sb.sem, lev_sb.after(l, n))
                        e.wait_ge(z_ok.sem, z_ok.after(l, n))
                        left = right = hg[:, Z0_ + n % 2, :]
                    for pair in range(HP):
                        for i in range(1 if n == 8 else TI):
                            for hh in range(2):
                                c, o = pair * SEQ + i * P, (pair * TI + i) * P
                                if n == 8:
                                    c, o = pair * SEQ, pair * P
                                cr = c + P if n == 8 else c
                                last = T.matmul(bank[4 + hh][:, o:o + P], left[64 * hh:64 * hh + 64, c:c + P],
                                                right[64 * hh:64 * hh + 64, cr:cr + P], start=True, stop=True)
                    last.then_inc(lev_ps.sem, 1)

                def qk_transposes(i):
                    if i:
                        e.wait_ge(qkt_sb.sem, qkt_sb.after(l, 2))
                    e.wait_ge(qk_ok.sem, qk_ok.after(l, i + 1))
                    for j in range(2):
                        for hd in range(HA):
                            last = T.transpose(bank[6 + j][:, hd * P:hd * P + P], qk[:, j, i, hd * P:hd * P + P], ident[:, :])
                        last.then_inc(qkt_ps.sem, 1)

                def scores(i):
                    e.wait_ge(qkt_sb.sem, qkt_sb.after(l, 2 * i + 2))
                    n = (i + 1) * P
                    for hd in range(HA):
                        for c in range(2):
                            b, o = (2 + c, hd * n) if i == 0 else (2 * c + hd // 2, hd % 2 * n)
                            last = T.matmul(bank[b][:, o:o + n], qkT[64 * c:64 * c + 64, hd, i * P:i * P + P],
                                            qkT[64 * c:64 * c + 64, HA + hd, 0:n], start=True, stop=True)
                    last.then_inc(sc_ps.sem, 1)

                def project_out(i, tiles):
                    for k in tiles:
                        for half in range(2):
                            W = ring[:, WOUT[half], :].rearrange("p (k n) -> p k n", k=KT)
                            last = T.matmul(bank[2 * i + half][:, :], mixT[:, k, i * P:i * P + P], W[:, k, :],
                                            start=(k == 6), stop=(k == 3))
                            if k == 3:
                                last.then_inc(op_ps.sem, 1)

                e.wait_ge(ht_sb.sem, ht_sb.after(l, 4))
                W = section(0)
                project_columns(W, 4, 0)
                project_columns(W, 5, 1)
                W = section(1)
                project_rows(W, 6, 0)
                project_rows(W, 7, 1)
                proj_read(2)
                level(0)
                W = section(2)
                project_rows(W, 0, 0)
                level(1)
                project_rows(W, 1, 1)
                level(2)
                W = section(3)
                project_rows(W, 2, 0)
                level(3)
                proj_read(4)
                qk_transposes(0)
                project_rows(W, 3, 1)
                level(4)
                W = section(4)
                proj_read(5)
                project_rows(W, 0, 0)
                level(5)
                qk_transposes(1)
                proj_read(6)
                project_rows(W, 1, 1)
                level(6)
                proj_read(8)
                scores(0)
                W = section(5)
                proj_read(9)
                project_columns(W, 0, 0)
                level(7)
                proj_read(10)
                project_columns(W, 1, 1)
                level(8)
                proj_read(12)
                e.wait_ge(exp_ok.sem, exp_ok.after(l, 1))
                scores(1)
                e.wait_ge(qkt_sb.sem, qkt_sb.after(l, 4))
                e.wait_ge(w_ok.sem, w_ok.after(l, 1))
                for hd in range(HA):
                    last = T.transpose(bank[7][:, hd * P:hd * P + P], att_w[:, hd, 0:P], ident[:, :])
                last.then_inc(wt_ps.sem, 1)
                W = section(6)
                project_columns(W, 6, 0)
                e.wait_ge(lev_sb.sem, lev_sb.after(l, 9))
                e.wait_ge(wt_sb.sem, wt_sb.after(l, 1))
                for hd in range(HA):
                    last = T.matmul(bank[5][:, hd * DV:hd * DV + DV], wT[:, hd, :], av[:, 0, hd * DV:hd * DV + DV],
                                    start=True, stop=True)
                last.then_inc(pv_ps.sem, 1)
                for i in range(TI):
                    for hd in range(HB):
                        pair, hh, o = hd // 2, hd % 2, (i * HB + hd) * DB
                        last = T.matmul(bank[7][:, o:o + DB], sT[:, hh, pair * TI + i, :],
                                        bib[:, i, hd * DB:hd * DB + DB], start=True, stop=(i == 0))
                        if i:
                            last = T.matmul(bank[7][:, o:o + DB], far[:, hh, pair, :],
                                            bib[:, 0, hd * DB:hd * DB + DB], start=False, stop=True)
                last.then_inc(ob_ps.sem, 1)

                def oa_transposes(i):
                    e.wait_ge(oa_ok.sem, oa_ok.after(l, i + 1))
                    for hd in range(HA):
                        last = T.transpose(bank[5 + i][:, hd * P:hd * P + P], oa[:, i, hd * P:hd * P + P], ident[:, :])
                    last.then_inc(oat_ps.sem, 1)

                e.wait_ge(w_ok.sem, w_ok.after(l, 2))
                proj_read(13)
                for hd in (0, 1):
                    for c in range(TI):
                        last = T.transpose(bank[6][:, (2 * hd + c) * P:(2 * hd + c) * P + P],
                                           att_w[:, hd, c * P:c * P + P], ident[:, :])
                last.then_inc(wt_ps.sem, 1)
                for hd in (2, 3):
                    for c in range(TI):
                        o = (2 * (hd - 2) + c) * P
                        last = T.transpose(bank[4][:, o:o + P], att_w[:, hd, c * P:c * P + P], ident[:, :])
                last.then_inc(wt_ps.sem, 1)
                oa_transposes(0)
                e.wait_ge(ring_full[1].sem, ring_full[1].after(l, 32))
                e.wait_ge(ring_full[2].sem, ring_full[2].after(l, 32))
                e.wait_ge(exp_ok.sem, exp_ok.after(l, 2))
                e.wait_ge(conv_ok.sem, conv_ok.after(l, 1))
                project_out(0, (6, 7))
                e.wait_ge(ob_ok.sem, ob_ok.after(l, 1))
                e.wait_ge(wt_sb.sem, wt_sb.after(l, 3))
                for hd in range(HA):
                    for c in range(2):
                        last = T.matmul(bank[7][:, hd * DV:hd * DV + DV], wT[:, 4 + 2 * hd + c, :],
                                        av[:, c, hd * DV:hd * DV + DV], start=(c == 0), stop=(c == 1))
                last.then_inc(pv_ps.sem, 1)
                for i in range(TI):
                    for c in range(2):
                        last = T.transpose(bank[4][:, (c * TI + i) * P:(c * TI + i) * P + P],
                                           ob[:, i * 256 + c * P:i * 256 + c * P + P], ident[:, :])
                last.then_inc(obt_ps.sem, 1)
                e.wait_ge(oat_sb.sem, oat_sb.after(l, 1))
                e.wait_ge(obt_sb.sem, obt_sb.after(l, 1))
                project_out(0, (4, 5, 0, 1, 2, 3))
                project_out(1, (6, 7, 4, 5))
                oa_transposes(1)
                e.wait_ge(oat_sb.sem, oat_sb.after(l, 2))
                project_out(1, (0, 1, 2, 3))

                transposed_rows(l, 1)
                e.wait_ge(ht_sb.sem, ht_sb.after(l, 8))
                for i in range(TI):
                    for k in range(KT):
                        last = T.matmul(bank[4][:, i * 64:i * 64 + NG + NE], hT[:, k, i * P:i * P + P], wr[:, k, :],
                                        start=(k == 0), stop=(k == KT - 1))
                last.then_inc(log_ps.sem, 1)
                e.wait_ge(picks_ok.sem, picks_ok.after(l, 1))
                T.matmul(bank[5][:, 0:NE], before[:, :], picks[:, 0, :], start=True, stop=True)
                T.matmul(bank[5][:, NE:2 * NE], before[:, :], picks[:, 1, :], start=True, stop=False)
                T.matmul(bank[5][:, NE:2 * NE], ones[:, :], picks[:, 0, :], start=False, stop=True)
                T.matmul(bank[5][:, 2 * NE:3 * NE], ones[:, :], picks[:, 0, :], start=True, stop=False)
                T.matmul(bank[5][:, 2 * NE:3 * NE], ones[:, :], picks[:, 1, :], start=False, stop=True).then_inc(rank_ps.sem, 1)

                with e.Fori(0, GROUPS) as g:
                    experts(main, l * GROUPS + g,
                            lambda s, i: ring_full[s].after(l, 16 * ((2 if s < 3 else 1) + i // 2 + 1)) + g * 32)
                count, prior = extra_groups(e, l)
                with e.If(count > 0):
                    with e.Fori(0, count) as t:
                        e.wait_ge(main.x_added.sem, main.x_added.after(l * GROUPS + GROUPS, 0))
                        experts(extra, prior + t, lambda s, i: xring_full[s].after(prior + t, 16 * (i // 2 + 1)))
                layer_sums(e, l, count, prior)

        @block.scalar
        def _(e):
            A = nc.scalar.activation
            e.wait_ge(pro_dve.sem, 2)
            A(lbt, lbt, ACT.Exp).then_inc(pro_act.sem, 1)
            e.wait_ge(pro_dve.sem, 3)
            A(sinb[:, :, :], ang.rearrange("p (i n) -> p i n", i=TI), ACT.Sin)
            A(cosb[:, :, :], angc.rearrange("p (i n) -> p i n", i=TI), ACT.Sin).then_inc(pro_act.sem, 1)
            e.wait_ge(x_in.sem, 16)

            def experts(S, turn):
                e.wait_ge(S.gat_ps.sem, S.gat_ps.after(turn, 1))
                A(gatT, bank[2][:, 0:TI * P], ACT.Copy).then_inc(S.gat_sb.sem, 1)
                for i in range(UG):
                    e.wait_ge(S.gu_ps.sem, S.gu_ps.after(turn, i + 1))
                    A(sil, bank[4][:, 0:P], ACT.Exp, scale=-1.0).then_inc(S.gu_exp.sem, 1)
                    e.wait_ge(S.at_ps.sem, S.at_ps.after(turn, i + 1))
                    A(actT, bank[3][:, 0:P], ACT.Copy).then_inc(S.at_sb.sem, 1)
                    e.wait_ge(S.ye_ps.sem, S.ye_ps.after(turn, i + 1))
                    for q in range(2):
                        last = A(ye[CAP * i:CAP * i + CAP, 2 * P * q:2 * P * q + 2 * P], bank[5][CAP * q:CAP * q + CAP, 0:2 * P], ACT.Copy)
                    last.then_inc(S.ye_act.sem, 1)

            with e.Fori(0, DEPTH) as l:

                def norm():
                    for i in range(TI):
                        A(smf[:, i * D:i * D + D], x[:, i, :], ACT.Square, accum_out=ssq[:, i:i + 1]).then_inc(sums_ok.sem, 1)

                def copy_out(n):
                    b = (4, 5, 6, 7, 0, 1, 2, 3, 0, 1, 0, 1, 6)[n - 1]
                    e.wait_ge(proj_ps.sem, proj_ps.after(l, n))
                    A(u[:, n - 1, :], bank[b][:, :], ACT.Copy).then_inc(proj_sb.sem, 1)

                def decays(n):
                    if n >= 3:
                        e.wait_ge(lev_ps.sem, lev_ps.after(l, n - 1))
                    e.wait_ge(z_diff.sem, z_diff.after(l, n))
                    Z = hg[:, Z0_ + n % 2, :]
                    if n == 8:
                        zv, dv, gv = (t.rearrange("p (h c t) -> p h c t", c=4, t=CHUNK) for t in (Z, hg[:, D_, :], hg[:, G_, :]))
                        A(zv[:, :, 0:2, :], dv[:, :, 0:2, :], ACT.Exp, scale=-1.0)
                        A(zv[:, :, 2, :], gv[:, :, 2, :], ACT.Exp)
                        A(zv[:, :, 3, :], dv[:, :, 3, :], ACT.Exp).then_inc(z_exp.sem, 1)
                        return
                    zv, dv, gv = (t.rearrange("p (b o t) -> p b o t", o=2, t=LEVELS[n]) for t in (Z, hg[:, D_, :], hg[:, G_, :]))
                    A(zv[:, :, 0, :], dv[:, :, 0, :], ACT.Exp, scale=-1.0)
                    A(zv[:, :, 1, :], (gv if LEVELS[n] == CHUNK else dv)[:, :, 1, :], ACT.Exp).then_inc(z_exp.sem, 1)

                def qk_squares(i):
                    e.wait_ge(proj_sb.sem, proj_sb.after(l, 5 + i))
                    if i:
                        e.wait_ge(qk_ok.sem, qk_ok.after(l, 1))
                    A(smf[:, 0:2 * 512].rearrange("p (j n) -> p j n", j=2), qk[:, :, i, :], ACT.Square).then_inc(qk_sq.sem, 1)

                def qkt_out(i):
                    for j in range(2):
                        e.wait_ge(qkt_ps.sem, qkt_ps.after(l, 2 * i + j + 1))
                        A(qkT[:, HA * j:HA * j + HA, i * P:i * P + P], bank[6 + j][:, :].rearrange("p (h c) -> p h c", h=HA),
                          ACT.Copy).then_inc(qkt_sb.sem, 1)

                def softmax_exp(i):
                    if i:
                        e.wait_ge(w_ok.sem, w_ok.after(l, 1))
                    e.wait_ge(max_ok.sem, max_ok.after(l, i + 1))
                    n = (i + 1) * P
                    for m in range(HC):
                        b, o = (2 + m // HA, m % HA * n) if i == 0 else (2 * (m // HA) + m % HA // 2, m % 2 * n)
                        last = A(sm[:, m, 0:n], bank[b][:, o:o + n], ACT.Exp, bias=negmax[:, i * HC + m:i * HC + m + 1],
                                 scale=DK ** -0.5, accum_out=denom[:, i * HC + m:i * HC + m + 1])
                    last.then_inc(exp_ok.sem, 1)

                def wt_out(n):
                    e.wait_ge(wt_ps.sem, wt_ps.after(l, n + 1))
                    A(wT[:, 4 * n:4 * n + 4, :], bank[(7, 6, 4)[n]][:, :].rearrange("p (h c) -> p h c", h=4), ACT.Copy).then_inc(wt_sb.sem, 1)

                def oa_squares(i):
                    e.wait_ge(pv_ps.sem, pv_ps.after(l, i + 1))
                    for hd in range(HA):
                        last = A(sq_junk[:, (4 * i + hd) * DV:(4 * i + hd + 1) * DV], bank[(5, 7)[i]][:, hd * DV:hd * DV + DV], ACT.Square,
                                 accum_out=oa_ms[:, 4 * i + hd:4 * i + hd + 1])
                    last.then_inc(oa_sq.sem, 1)

                norm()
                copy_out(1)
                e.wait_ge(proj_sb.sem, proj_sb.after(l, 1))
                A(hg[:, Z0_, :], bq, ACT.Exp, scale=-1.0).then_inc(hg_act.sem, 1)
                copy_out(2)
                e.wait_ge(hg_dve.sem, hg_dve.after(l, 1))
                A(hg[:, Z0_ + 1, :], hg[:, D_, :], ACT.Exp, scale=-1.0).then_inc(hg_act.sem, 1)
                e.wait_ge(hg_dve.sem, hg_dve.after(l, 2))
                A(hg[:, G_, :], hg[:, G_, :], ACT.Ln)
                A(hg[:, Z0_, :], hg[:, Z0_, :], ACT.Ln, scale=1.0 / LN_CUT).then_inc(hg_act.sem, 1)
                e.wait_ge(lam_sum.sem, lam_sum.after(l, 1))
                A(lam_e, lam_s, ACT.Exp).then_inc(lam_exp.sem, 1)
                copy_out(3)
                copy_out(4)
                decays(1)
                decays(2)
                copy_out(5)
                qk_squares(0)
                decays(3)
                copy_out(6)
                decays(4)
                qk_squares(1)
                copy_out(7)
                decays(5)
                qkt_out(0)
                copy_out(8)
                decays(6)
                copy_out(9)
                decays(7)
                qkt_out(1)
                copy_out(10)
                decays(8)
                e.wait_ge(proj_sb.sem, proj_sb.after(l, 10))
                e.wait_ge(z_exp.sem, z_exp.after(l, 8))
                A(egate.rearrange("p (i n) -> p i n", i=TI), bib[:, :, HB * DB:2 * HB * DB], ACT.Exp, scale=-1.0).then_inc(gate_exp.sem, 1)
                softmax_exp(0)
                copy_out(11)
                copy_out(12)
                wt_out(0)
                softmax_exp(1)
                copy_out(13)
                oa_squares(0)
                e.wait_ge(conv_in.sem, conv_in.after(l, 1))
                for back, tap in ((0, cxT), (1, bq), (2, bf)):
                    for ct in range(2):
                        w = 4 + 2 * (2 - back) + ct
                        last = A(tap[:, ct * SEQ:ct * SEQ + SEQ], ccT[:, ct * SEQ:ct * SEQ + SEQ], ACT.Copy, scale=cur[:, w:w + 1])
                last.then_inc(taps_ok.sem, 1)
                e.wait_ge(ob_ps.sem, ob_ps.after(l, 1))
                for m in range(TI * HB):
                    last = A(sq_junk[:, 8 * DV + m * DB:8 * DV + m * DB + DB], bank[7][:, m * DB:m * DB + DB], ACT.Square, accum_out=ob_ms[:, m:m + 1])
                last.then_inc(ob_sq.sem, 1)
                wt_out(1)
                wt_out(2)

                def oat_out(i):
                    e.wait_ge(oat_ps.sem, oat_ps.after(l, i + 1))
                    A(mixT[:, 0:4, i * P:i * P + P], bank[5 + i][:, :].rearrange("p (h c) -> p h c", h=4), ACT.Copy).then_inc(oat_sb.sem, 1)

                oat_out(0)
                oa_squares(1)
                e.wait_ge(obt_ps.sem, obt_ps.after(l, 1))
                A(mixT[:, 4:6, :], bank[4][:, :].rearrange("p (c t) -> p c t", c=2), ACT.Copy).then_inc(obt_sb.sem, 1)
                oat_out(1)
                for i in range(TI):
                    e.wait_ge(x_mixed.sem, x_mixed.after(l, 2 * i + 2))
                    A(smf[:, i * D:i * D + D], x[:, i, :], ACT.Square, accum_out=ssq[:, i:i + 1]).then_inc(sums_ok.sem, 1)
                e.wait_ge(top_g.sem, top_g.after(l, 1))
                for i in range(TI):
                    last = A(rjunk[:, i, :], lg[:, i, 0:NG], ACT.Exp, bias=nmg[:, i:i + 1], accum_out=expsum[:, i:i + 1])
                last.then_inc(exp_g.sem, 1)
                e.wait_ge(top_e.sem, top_e.after(l, 1))
                A(edif, edif, ACT.Exp).then_inc(exp_e.sem, 1)

                e.wait_ge(routed.sem, routed.after(l, 1))
                settle(e)
                with e.If(l < DEPTH - 1):
                    layer_parameters(e, nc.s_assert_within(l + 1, 1, DEPTH - 1))
                with e.Fori(0, GROUPS) as g:
                    experts(main, l * GROUPS + g)
                count, prior = extra_groups(e, l)
                with e.If(count > 0):
                    with e.Fori(0, count) as t:
                        e.wait_ge(main.x_added.sem, main.x_added.after(l * GROUPS + GROUPS, 0))
                        experts(extra, prior + t)
                layer_sums(e, l, count, prior)

        @block.vector
        def _(e):
            V = nc.vector
            TT, TS, STT = V.tensor_tensor, V.tensor_scalar, V.scalar_tensor_tensor
            for S in (main, extra):
                e.sem_inc(S.x_added.sem, 1)
                e.sem_inc(S.dve.sem, 1)
            c = Chain(pro_dve, 0)
            e.wait_ge(pro_pe.sem, 1)
            V.tensor_copy(pcol[:, :], bank[0][:, 0:DEPTH * 8]).then_inc(c.step(), 1)
            e.wait_ge(c.sem, c.last())
            lb_raw = pcol[:, 0:DEPTH * HP].rearrange("p (l h) -> p h l", l=DEPTH)
            lbl = lbt.rearrange("p (l h) -> p l h", l=DEPTH)
            e.wait_ge(const_ok.sem, CONSTS)
            prol = Chain(dve_p, 0)
            V.tensor_reduce(lbm, lb_raw, AX, ALU.max).then_inc(prol.step(), 1)
            e.wait_ge(prol.sem, prol.last())
            TT(lbl, pcol[:, 0:DEPTH * HP].rearrange("p (l h) -> p l h", l=DEPTH), lbm.unsqueeze(1).to_broadcast([P, DEPTH, HP]), ALU.subtract).then_inc(c.step(), 1)
            e.wait_ge(pos_in.sem, 16)
            angv, turnv, angcv = (t.rearrange("p (i n) -> p i n", i=TI) for t in (ang, turn_n, angc))
            V.tensor_copy(pos_f, pos_i[:, :]).then_inc(prol.step(), 1)
            e.wait_ge(prol.sem, prol.last())
            TT(angv, pos_f.unsqueeze(2).to_broadcast([P, TI, HALF]), freq.unsqueeze(1).to_broadcast([P, TI, HALF]), ALU.mult).then_inc(prol.step(), 1)
            e.wait_ge(prol.sem, prol.last())
            TS(turn_n, ang, 1.0 / (2 * math.pi), 12582912.0, ALU.mult, ALU.add).then_inc(prol.step(), 1)
            e.wait_ge(prol.sem, prol.last())
            TS(turn_n, turn_n, -12582912.0, None, ALU.add).then_inc(prol.step(), 1)
            e.wait_ge(prol.sem, prol.last())
            parts, rest = [6.25, 0.03125], 2 * math.pi - 6.25 - 0.03125
            parts.append(math.floor(rest * 2 ** 17) / 2 ** 17)
            parts.append(rest - parts[-1])
            for part in parts:
                STT(ang, turn_n, -part, ang, ALU.mult, ALU.add).then_inc(prol.step(), 1)
                e.wait_ge(prol.sem, prol.last())
            PI = 3.1415925
            TS(angc, ang, math.pi / 2, None, ALU.add).then_inc(prol.step(), 1)
            TS(ang, ang, PI, -PI, ALU.min, ALU.max).then_inc(prol.step(), 1)
            e.wait_ge(prol.sem, prol.last())
            TS(turn_n, angc, math.pi, -2 * math.pi, ALU.is_gt, ALU.mult).then_inc(prol.step(), 1)
            e.wait_ge(prol.sem, prol.last())
            TT(angc, angc, turn_n, ALU.add).then_inc(prol.step(), 1)
            e.wait_ge(prol.sem, prol.last())
            TS(angc, angc, PI, -PI, ALU.min, ALU.max).then_inc(c.step(), 1)
            e.wait_ge(pro_act.sem, 1)
            V.tensor_reduce(lbs, lbt.rearrange("p (l h) -> p h l", l=DEPTH), AX, ALU.add).then_inc(prol.step(), 1)
            V.memset(table[:, 0, 0:HP], 0.0).then_inc(prol.step(), 1)
            e.wait_ge(prol.sem, prol.last())
            V.reciprocal(lbs, lbs).then_inc(prol.step(), 1)
            e.wait_ge(prol.sem, prol.last())
            TT(lbl, lbl, lbs.unsqueeze(1).to_broadcast([P, DEPTH, HP]), ALU.mult).then_inc(prol.step(), 1)
            e.wait_ge(prol.sem, prol.last())
            for n in range(1, DEPTH):
                TT(table[:, n, 0:HP], table[:, n - 1, 0:HP], lbl[:, n, :], ALU.add).then_inc(prol.step(), 1)
                e.wait_ge(prol.sem, prol.last())
            TS(table[:, :, HP:2 * HP], table[:, :, 0:HP], -1.0, 1.0, ALU.mult, ALU.add).then_inc(prol.step(), 1)
            V.tensor_copy(table[:, :, 4:10], pcol[:, DEPTH * HP:DEPTH * 8].rearrange("p (l j) -> p l j", l=DEPTH)).then_inc(prol.step(), 1)
            e.wait_ge(prol.sem, prol.last())
            e.wait_ge(pro_act.sem, 2)

            def experts(S, turn, meanwhile=None):
                c = Chain(S.dve, turn)
                e.wait_ge(c.sem, c.last())
                for i in range(TI):
                    TS(sel[:, i, :], iota[:, :], codes[:, i:i + 1], None, ALU.is_equal).then_inc(c.step(), 1)
                    TS(gat[:, i, :], iota[:, :], codes[:, i:i + 1], gates[:, i:i + 1], ALU.is_equal, ALU.mult).then_inc(c.step(), 1)
                    TS(gtmp[:, i, :], iota[:, :], codes[:, TI + i:TI + i + 1], gates[:, TI + i:TI + i + 1], ALU.is_equal, ALU.mult).then_inc(c.step(), 1)
                e.wait_ge(c.sem, c.last())
                for i in range(TI):
                    STT(sel[:, i, :], iota[:, :], codes[:, TI + i:TI + i + 1], sel[:, i, :], ALU.is_equal, ALU.add).then_inc(c.step(), 1)
                TT(gat, gat, gtmp, ALU.add).then_inc(S.sel_ok.sem, 1)
                e.wait_ge(c.sem, c.last())
                TS(codes, codes, -float(UG * CAP), None, ALU.add).then_inc(c.step(), 1)
                if meanwhile:
                    meanwhile()
                for half in range(2):
                    e.wait_ge(S.gath_ps.sem, S.gath_ps.after(turn, half + 1))
                    TT(xg[:, 4 * half:4 * half + 4, :], bank[half][:, :].rearrange("p (k c) -> p k c", k=4),
                       gffn[:, 4 * half:4 * half + 4].unsqueeze(2).to_broadcast([P, 4, P]), ALU.mult).then_inc(S.xg_ok.sem, 1)
                for i in range(UG):
                    e.wait_ge(S.gu_exp.sem, S.gu_exp.after(turn, i + 1))
                    TS(silr, sil, 1.0, None, ALU.add).then_inc(c.step(), 1)
                    e.wait_ge(c.sem, c.last())
                    V.reciprocal(silr, silr).then_inc(c.step(), 1)
                    e.wait_ge(c.sem, c.last())
                    TT(silr, bank[4][:, 0:P], silr, ALU.mult).then_inc(c.step(), 1)
                    e.wait_ge(c.sem, c.last())
                    TT(actv, bank[4][:, P:2 * P], silr, ALU.mult).then_inc(S.act_ok.sem, 1)
                    e.wait_ge(S.ye_ps.sem, S.ye_ps.after(turn, i + 1))
                    for q in range(2, 4):
                        last = V.tensor_copy(ye[CAP * i:CAP * i + CAP, 2 * P * q:2 * P * q + 2 * P], bank[5][CAP * q:CAP * q + CAP, 0:2 * P])
                    last.then_inc(S.ye_dve.sem, 1)
                for n in range(4):
                    e.wait_ge(S.scat_ps.sem, S.scat_ps.after(turn, n + 1))
                    xs = x[:, n // 2, n % 2 * 512:n % 2 * 512 + 512]
                    TT(xs, bank[6 + n % 2][:, :], xs, ALU.add).then_inc(S.x_added.sem, 1)
                c.end()

            e.wait_ge(x_in.sem, 16)
            with e.Fori(0, DEPTH) as l:
                c = Chain(dve_m, l)

                def rsqrt(dst, sums, n):
                    m = sums.shape[1]
                    v, vh, w = rs_v[:, 0:m], rs_h[:, 0:m], rs_w[:, 0:m]
                    TS(v, sums, 1.0 / n, EPS, ALU.mult, ALU.add).then_inc(c.step(), 1)
                    TS(vh, sums, -0.5 / n, -0.5 * EPS, ALU.mult, ALU.add).then_inc(c.step(), 1)
                    e.wait_ge(c.sem, c.last())
                    TS(dst.bitcast(I32), v.bitcast(I32), -0.5, float(0x5F3759DF), ALU.mult, ALU.add).then_inc(c.step(), 1)
                    for _ in range(3):
                        e.wait_ge(c.sem, c.last())
                        TT(w, dst, dst, ALU.mult).then_inc(c.step(), 1)
                        e.wait_ge(c.sem, c.last())
                        TT(w, w, vh, ALU.mult).then_inc(c.step(), 1)
                        e.wait_ge(c.sem, c.last())
                        STT(dst, w, 1.5, dst, ALU.add, ALU.mult).then_inc(c.step(), 1)
                    e.wait_ge(c.sem, c.last())

                def norm(which, gain):
                    for i in range(TI):
                        if which:
                            for half in range(2):
                                e.wait_ge(op_ps.sem, op_ps.after(l, 2 * i + half + 1))
                                xs = x[:, i, half * 512:half * 512 + 512]
                                TT(xs, bank[2 * i + half][:, :], xs, ALU.add).then_inc(x_mixed.sem, 1)
                        e.wait_ge(sums_ok.sem, sums_ok.after(l, 2 * which + i + 1))
                        rsqrt(rstd[:, i:i + 1], ssq[:, i:i + 1], D)
                        TS(h[:, i, :, :], x[:, i, :].rearrange("p (c k) -> p k c", k=KT), rstd[:, i:i + 1], None,
                           ALU.mult).then_inc(h_ok.sem, 1)
                    if which == 0:
                        e.wait_ge(params_in.sem, params_in.after(l, 16 * 14))
                        start_of_layer()
                    for n in range(4):
                        i, half = n // 2, n % 2
                        e.wait_ge(ht_ps.sem, ht_ps.after(l, 4 * which + n + 1))
                        TT(hT[:, 4 * half:4 * half + 4, i * P:i * P + P], bank[n][:, :].rearrange("p (k c) -> p k c", k=4),
                           gain[:, 4 * half:4 * half + 4].unsqueeze(2).to_broadcast([P, 4, P]), ALU.mult).then_inc(ht_sb.sem, 1)

                def start_of_layer():
                    V.tensor_copy(cur[:, :].unsqueeze(1), table[:, ds(l, 1), :]).then_inc(c.step(), 1)
                    V.memset(sT[:, :, :, :], 0.0).then_inc(c.step(), 1)
                    V.tensor_copy(gffn[:, :], gffn_in[:, :]).then_inc(c.step(), 1)
                    lv = lamv[:, :, :].rearrange("p (a b) n -> p a b n", b=2)
                    prod = smf[:, 0:2 * DK].rearrange("p (a n) -> p a n", a=2)
                    TT(prod, lv[:, :, 0, :], lv[:, :, 1, :], ALU.mult).then_inc(c.step(), 1)
                    e.wait_ge(c.sem, c.last())
                    V.tensor_reduce(lam_s, prod, AX, ALU.add).then_inc(lam_sum.sem, 1)
                    TS(subs, cur[:, 10:11], -1.0, 1.0, ALU.mult, ALU.add).then_inc(c.step(), 1)
                    e.wait_ge(c.sem, c.last())
                    TS(subgl[:, :], subg[:, :], subs, None, ALU.mult).then_inc(c.step(), 1)

                def hgrn_inputs():
                    G, Q, K, Dt, A0, A1 = (hg[:, n, :] for n in range(6))
                    e.wait_ge(hg_act.sem, hg_act.after(l, 1))
                    TS(A0, A0, 1.0, None, ALU.add).then_inc(c.step(), 1)
                    e.wait_ge(c.sem, c.last())
                    V.reciprocal(A0, A0).then_inc(c.step(), 1)
                    e.wait_ge(proj_sb.sem, proj_sb.after(l, 2))
                    TS(Dt, bf, -80.0, None, ALU.max).then_inc(hg_dve.sem, 1)
                    e.wait_ge(c.sem, c.last())
                    TT(Q, bq, A0, ALU.mult).then_inc(c.step(), 1)
                    e.wait_ge(hg_act.sem, hg_act.after(l, 2))
                    e.wait_ge(c.sem, c.last())
                    TS(A0, A1, 1.0, None, ALU.add).then_inc(c.step(), 1)
                    e.wait_ge(c.sem, c.last())
                    V.reciprocal(A0, A0).then_inc(c.step(), 1)
                    e.wait_ge(c.sem, c.last())
                    TT(A1, A1, A0, ALU.mult).then_inc(c.step(), 1)
                    for p in range(HP):
                        s = slice(p * SEQ, p * SEQ + SEQ)
                        TS(Dt[:, s], A0[:, s], cur[:, HP + p:HP + p + 1], cur[:, p:p + 1], ALU.mult, ALU.add).then_inc(c.step(), 1)
                    e.wait_ge(c.sem, c.last())
                    TS(G, Dt, LN_CUT, None, ALU.max).then_inc(c.step(), 1)
                    TS(A0, Dt, TINY, LN_CUT, ALU.max, ALU.min).then_inc(hg_dve.sem, 1)
                    for p in range(HP):
                        s = slice(p * SEQ, p * SEQ + SEQ)
                        last = TS(K[:, s], A1[:, s], cur[:, HP + p:HP + p + 1], None, ALU.mult)
                        if p < HP - 1:
                            last.then_inc(c.step(), 1)
                    last.then_inc(hg_qk.sem, 1)
                    e.wait_ge(hg_act.sem, hg_act.after(l, 3))
                    TT(Dt, G, A0, ALU.add).then_inc(c.step(), 1)
                    e.wait_ge(c.sem, c.last())
                    V.tensor_tensor_scan(out=G, data0=restart[:, :, :].rearrange("p h t -> p (h t)"), data1=Dt,
                                         initial=0.0, op0=ALU.mult, op1=ALU.add).then_inc(c.step(), 1)
                    e.wait_ge(c.sem, c.last())

                def differences(n):
                    if n > 1:
                        e.wait_ge(z_exp.sem, z_exp.after(l, n - 1))
                    if n == 8:
                        gv, dv = (t.rearrange("p (h c t) -> p h c t", c=4, t=CHUNK) for t in (hg[:, G_, :], hg[:, D_, :]))
                        TT(dv[:, :, 0:2, :], gv[:, :, 0:2, :], gv[:, :, 0:2, CHUNK - 1:CHUNK].to_broadcast([P, HP, 2, CHUNK]), ALU.subtract).then_inc(c.step(), 1)
                        e.wait_ge(c.sem, c.last())
                        TT(dv[:, :, 0, :], dv[:, :, 0, :], gv[:, :, 1, CHUNK - 1:CHUNK].to_broadcast([P, HP, CHUNK]), ALU.subtract).then_inc(c.step(), 1)
                        TT(dv[:, :, 3, :], gv[:, :, 3, :], gv[:, :, 2, CHUNK - 1:CHUNK].to_broadcast([P, HP, CHUNK]), ALU.add).then_inc(z_diff.sem, 1)
                        return
                    B = LEVELS[n]
                    nb = HP * SEQ // (2 * B)
                    gv, dv = (t.rearrange("p (b t) -> p b t", t=2 * B) for t in (hg[:, G_, :], hg[:, D_, :]))
                    w = B if B == CHUNK else 2 * B
                    TT(dv[:, :, 0:w], gv[:, :, 0:w], gv[:, :, B - 1:B].to_broadcast([P, nb, w]), ALU.subtract).then_inc(z_diff.sem, 1)

                def scaled(n):
                    e.wait_ge(z_exp.sem, z_exp.after(l, n))
                    Z = hg[:, Z0_ + n % 2, :]
                    if n == 8:
                        zv, kv, qv = (t.rearrange("p (h c t) -> p h c t", c=2, t=P) for t in (Z, hg[:, KEY_, :], hg[:, Q_, :]))
                    else:
                        zv, kv, qv = (t.rearrange("p (b o t) -> p b o t", o=2, t=LEVELS[n]) for t in (Z, hg[:, KEY_, :], hg[:, Q_, :]))
                    TT(zv[:, :, 0, :], zv[:, :, 0, :], kv[:, :, 0, :], ALU.mult).then_inc(c.step(), 1)
                    TT(zv[:, :, 1, :], zv[:, :, 1, :], qv[:, :, 1, :], ALU.mult).then_inc(z_ok.sem, 1)

                def take_level(n):
                    e.wait_ge(lev_ps.sem, lev_ps.after(l, n + 1))
                    settle(e)
                    for hh in range(2):
                        if n == 8:
                            last = V.tensor_copy(far[:, hh, :, :], bank[4 + hh][:, 0:HP * P].rearrange("p (h t) -> p h t", h=HP))
                        else:
                            last = V.copy_predicated(sT[:, hh, :, :], masks[:, n:n + 1, :].bitcast(I32).to_broadcast([P, HP * TI, P]),
                                                     bank[4 + hh][:, :].rearrange("p (h t) -> p h t", t=P))
                        if hh == 0:
                            last.then_inc(c.step(), 1)
                    last.then_inc(lev_sb.sem, 1)

                def qk_finish(i):
                    e.wait_ge(qk_sq.sem, qk_sq.after(l, i + 1))
                    V.tensor_reduce(qk_ms, smf[:, 0:2 * 512].rearrange("p (m d) -> p m d", d=DK), AX, ALU.add).then_inc(c.step(), 1)
                    e.wait_ge(c.sem, c.last())
                    rsqrt(qk_rs, qk_ms, DK)
                    v = qk[:, :, i, :].rearrange("p j (m d) -> p j m d", d=DK)
                    TT(v, v, qk_rs.rearrange("p (j m) -> p j m", j=2).unsqueeze(3).to_broadcast([P, 2, HC, DK]), ALU.mult).then_inc(c.step(), 1)
                    e.wait_ge(c.sem, c.last())
                    TT(v, v, qkg[:, :, :].unsqueeze(2).to_broadcast([P, 2, HC, DK]), ALU.mult).then_inc(c.step(), 1)
                    e.wait_ge(c.sem, c.last())
                    t1, t2 = v[:, :, :, 0:HALF], v[:, :, :, HALF:2 * HALF]
                    w = 2 * HC * HALF
                    t1c, t2s, t1s, t2c = (smf[:, n * w:n * w + w].rearrange("p (j m d) -> p j m d", j=2, d=HALF) for n in range(4))
                    cv, sv = (t[:, i:i + 1, :].unsqueeze(1).to_broadcast([P, 2, HC, HALF]) for t in (cosb, sinb))
                    TT(t1c, t1, cv, ALU.mult).then_inc(c.step(), 1)
                    TT(t2s, t2, sv, ALU.mult).then_inc(c.step(), 1)
                    TT(t1s, t1, sv, ALU.mult).then_inc(c.step(), 1)
                    TT(t2c, t2, cv, ALU.mult).then_inc(c.step(), 1)
                    e.wait_ge(c.sem, c.last())
                    TT(t1, t1c, t2s, ALU.subtract).then_inc(c.step(), 1)
                    TT(t2, t1s, t2c, ALU.add).then_inc(qk_ok.sem, 1)

                def softmax_max(i):
                    e.wait_ge(sc_ps.sem, sc_ps.after(l, i + 1))
                    n = (i + 1) * P
                    banks = (2, 3) if i == 0 else (0, 1, 2, 3)
                    maps = HC // len(banks)
                    for b in banks:
                        v = bank[b][:, :].rearrange("p (m n) -> p m n", m=maps)[:, :, n - CHUNK:n]
                        TT(v, v, attn_mask[:, :].unsqueeze(1).to_broadcast([P, maps, CHUNK]), ALU.add).then_inc(c.step(), 1)
                    e.wait_ge(c.sem, c.last())
                    nm = negmax[:, i * HC:i * HC + HC]
                    for m, b in enumerate(banks):
                        V.tensor_reduce(nm[:, m * maps:m * maps + maps], bank[b][:, :].rearrange("p (m n) -> p m n", m=maps), AX, ALU.max).then_inc(c.step(), 1)
                    e.wait_ge(c.sem, c.last())
                    TS(nm, nm, -DK ** -0.5, None, ALU.mult).then_inc(max_ok.sem, 1)

                def attention_weights(i):
                    e.wait_ge(exp_ok.sem, exp_ok.after(l, i + 1))
                    n, r = (i + 1) * P, inv[:, i * HC:i * HC + HC]
                    V.reciprocal(r, denom[:, i * HC:i * HC + HC]).then_inc(c.step(), 1)
                    e.wait_ge(c.sem, c.last())
                    TS(r[:, HA:HC], r[:, HA:HC], nlam, None, ALU.mult).then_inc(c.step(), 1)
                    e.wait_ge(c.sem, c.last())
                    TT(sm[:, :, 0:n], sm[:, :, 0:n], r.unsqueeze(2).to_broadcast([P, HC, n]), ALU.mult).then_inc(c.step(), 1)
                    if i:
                        e.wait_ge(wt_ps.sem, wt_ps.after(l, 1))
                    e.wait_ge(c.sem, c.last())
                    TT(att_w[:, :, 0:n], sm[:, 0:HA, 0:n], sm[:, HA:HC, 0:n], ALU.add).then_inc(w_ok.sem, 1)

                def oa_finish(i):
                    e.wait_ge(oa_sq.sem, oa_sq.after(l, i + 1))
                    rs = oa_rs[:, 4 * i:4 * i + 4]
                    rsqrt(rs, oa_ms[:, 4 * i:4 * i + 4], DV)
                    v = oa[:, i, :].rearrange("p (h d) -> p h d", d=DV)
                    TT(v, bank[(5, 7)[i]][:, :].rearrange("p (h d) -> p h d", d=DV),
                       rs.unsqueeze(2).to_broadcast([P, HA, DV]), ALU.mult).then_inc(c.step(), 1)
                    e.wait_ge(c.sem, c.last())
                    TT(v, v, subgl[:, :].unsqueeze(1).to_broadcast([P, HA, DV]), ALU.mult).then_inc(oa_ok.sem, 1)

                norm(0, gmix)
                hgrn_inputs()
                differences(1)
                differences(2)
                scaled(1)
                scaled(2)
                take_level(0)
                differences(3)
                take_level(1)
                differences(4)
                qk_finish(0)
                scaled(3)
                take_level(2)
                differences(5)
                scaled(4)
                qk_finish(1)
                take_level(3)
                differences(6)
                scaled(5)
                take_level(4)
                differences(7)
                scaled(6)
                take_level(5)
                differences(8)
                scaled(7)
                take_level(6)
                scaled(8)
                e.wait_ge(lam_exp.sem, lam_exp.after(l, 1))
                TT(nlam, lam_e[:, 1:2], lam_e[:, 0:1], ALU.subtract).then_inc(c.step(), 1)
                e.wait_ge(c.sem, c.last())
                TT(nlam, nlam, cur[:, 10:11], ALU.subtract).then_inc(c.step(), 1)
                softmax_max(0)
                take_level(7)
                attention_weights(0)
                take_level(8)
                e.wait_ge(gate_exp.sem, gate_exp.after(l, 1))
                gview = egate.rearrange("p (i n) -> p i n", i=TI)
                TS(egate, egate, 1.0, None, ALU.add).then_inc(c.step(), 1)
                softmax_max(1)
                V.reciprocal(egate, egate).then_inc(c.step(), 1)
                e.wait_ge(c.sem, c.last())
                TT(gview, gview, bib[:, :, HB * DB:2 * HB * DB], ALU.mult).then_inc(c.step(), 1)
                attention_weights(1)
                oa_finish(0)
                e.wait_ge(ob_sq.sem, ob_sq.after(l, 1))
                rsqrt(ob_rs, ob_ms, DB)
                obv = ob.rearrange("p (m d) -> p m d", d=DB)
                TT(obv, bank[7][:, :].rearrange("p (m d) -> p m d", d=DB), ob_rs.unsqueeze(2).to_broadcast([P, TI * HB, DB]),
                   ALU.mult).then_inc(c.step(), 1)
                e.wait_ge(c.sem, c.last())
                TT(obv, obv, hng[:, :].unsqueeze(1).to_broadcast([P, TI * HB, DB]), ALU.mult).then_inc(c.step(), 1)
                e.wait_ge(c.sem, c.last())
                TT(ob, ob, egate, ALU.mult).then_inc(ob_ok.sem, 1)
                oa_finish(1)
                norm(1, gffn)
                e.wait_ge(log_ps.sem, log_ps.after(l, 1))
                logits = bank[4][:, 0:TI * 64].rearrange("p (i n) -> p i n", i=TI)
                V.memset(lg[:, :, NG:8], -3.0e38).then_inc(c.step(), 1)
                TT(lg[:, :, 0:NG], logits[:, :, 0:NG], rb[:, 0:NG].unsqueeze(1).to_broadcast([P, TI, NG]), ALU.add).then_inc(c.step(), 1)
                TT(lg[:, :, 8:8 + NE], logits[:, :, NG:NG + NE], rb[:, NG:NG + NE].unsqueeze(1).to_broadcast([P, TI, NE]), ALU.add).then_inc(c.step(), 1)
                e.wait_ge(c.sem, c.last())
                settle(e)
                for i in range(TI):
                    V.max(mg[:, i, :], lg[:, i, 0:8]).then_inc(c.step(), 1)
                e.wait_ge(c.sem, c.last())
                settle(e)
                for i in range(TI):
                    V.max_index(idx[:, i, :], mg[:, i, :], lg[:, i, 0:8]).then_inc(c.step(), 1)
                TS(nmg, mg[:, :, 0], -1.0, None, ALU.mult).then_inc(top_g.sem, 1)
                e.wait_ge(c.sem, c.last())
                V.tensor_copy(gidx, idx[:, 0:TI, 0]).then_inc(c.step(), 1)
                e.wait_ge(c.sem, c.last())
                TT(ohg, iota[:, 0:NG].unsqueeze(1).to_broadcast([P, TI, NG]), gidx.unsqueeze(2).to_broadcast([P, TI, NG]), ALU.is_equal).then_inc(c.step(), 1)
                e.wait_ge(c.sem, c.last())
                TS(pen, ohg, 1.0e30, -1.0e30, ALU.mult, ALU.add).then_inc(c.step(), 1)
                lge = lg[:, :, 8:8 + NE].rearrange("p i (g n) -> p i g n", g=NG)
                emv = em.rearrange("p i (g n) -> p i g n", g=NG)
                TT(emv, lge, ohg.unsqueeze(3).to_broadcast([P, TI, NG, EPG]), ALU.mult).then_inc(c.step(), 1)
                e.wait_ge(c.sem, c.last())
                TT(emv, emv, pen.unsqueeze(3).to_broadcast([P, TI, NG, EPG]), ALU.add).then_inc(c.step(), 1)
                e.wait_ge(c.sem, c.last())
                settle(e)
                for i in range(TI):
                    V.max(mv[:, i, :], em[:, i, :]).then_inc(c.step(), 1)
                e.wait_ge(c.sem, c.last())
                settle(e)
                for i in range(TI):
                    V.max_index(idx[:, TI + i, :], mv[:, i, :], em[:, i, :]).then_inc(c.step(), 1)
                TT(edif, mv[:, :, 1], mv[:, :, 0], ALU.subtract).then_inc(top_e.sem, 1)
                e.wait_ge(c.sem, c.last())
                V.tensor_copy(eid, idx[:, TI:2 * TI, 0:NK].rearrange("p i k -> p k i")).then_inc(c.step(), 1)
                e.wait_ge(c.sem, c.last())
                TT(oh, iota[:, 0:NE].unsqueeze(1).to_broadcast([P, NK * TI, NE]),
                   eidf.unsqueeze(2).to_broadcast([P, NK * TI, NE]), ALU.is_equal).then_inc(c.step(), 1)
                e.wait_ge(c.sem, c.last())
                TT(picks, oh[:, 0:TI, :], oh[:, TI:2 * TI, :], ALU.add).then_inc(picks_ok.sem, 1)
                e.wait_ge(exp_g.sem, exp_g.after(l, 1))
                e.wait_ge(exp_e.sem, exp_e.after(l, 1))
                TS(gates[:, TI:2 * TI], edif, 1.0, None, ALU.add).then_inc(c.step(), 1)
                e.wait_ge(c.sem, c.last())
                TT(gates[:, TI:2 * TI], gates[:, TI:2 * TI], expsum, ALU.mult).then_inc(c.step(), 1)
                e.wait_ge(c.sem, c.last())
                V.reciprocal(gates[:, 0:TI], gates[:, TI:2 * TI]).then_inc(c.step(), 1)
                e.wait_ge(c.sem, c.last())
                TT(gates[:, TI:2 * TI], gates[:, 0:TI], edif, ALU.mult).then_inc(c.step(), 1)
                e.wait_ge(rank_ps.sem, rank_ps.after(l, 1))
                V.tensor_copy(ranks, bank[5][:, 0:3 * NE]).then_inc(c.step(), 1)
                e.wait_ge(c.sem, c.last())
                rk = ranks[:, 0:TI * NE].rearrange("p (i n) -> p i n", i=TI)
                for k in range(NK):
                    TT(prod4[:, TI * k:TI * k + TI, :], oh[:, TI * k:TI * k + TI, :], rk, ALU.mult).then_inc(c.step(), 1)
                counts = ranks[:, TI * NE:3 * NE]
                TT(over, counts.unsqueeze(2).to_broadcast([P, NE, SEQ // CAP - 1]),
                   thr_cap.unsqueeze(1).to_broadcast([P, NE, SEQ // CAP - 1]), ALU.is_gt).then_inc(c.step(), 1)
                e.wait_ge(c.sem, c.last())
                V.tensor_reduce(rank4, prod4, AX, ALU.add).then_inc(c.step(), 1)
                V.tensor_reduce(units, over, AX, ALU.add).then_inc(c.step(), 1)
                e.wait_ge(c.sem, c.last())
                V.tensor_tensor_scan(out=upto, data0=ones[:, 0:NE], data1=units, initial=0.0, op0=ALU.mult, op1=ALU.add).then_inc(c.step(), 1)
                e.wait_ge(c.sem, c.last())
                TT(units, upto, units, ALU.subtract).then_inc(c.step(), 1)
                e.wait_ge(c.sem, c.last())
                TT(prod4, oh, units.unsqueeze(1).to_broadcast([P, NK * TI, NE]), ALU.mult).then_inc(c.step(), 1)
                e.wait_ge(c.sem, c.last())
                V.tensor_reduce(base4, prod4, AX, ALU.add).then_inc(c.step(), 1)
                TS(full4, rank4, float(CAP), None, ALU.is_ge).then_inc(c.step(), 1)
                e.wait_ge(c.sem, c.last())
                STT(base4, base4, float(NE - 1), eidf, ALU.add, ALU.subtract).then_inc(c.step(), 1)
                e.wait_ge(c.sem, c.last())
                TT(base4, base4, full4, ALU.mult).then_inc(c.step(), 1)
                e.wait_ge(c.sem, c.last())
                TT(base4, base4, eidf, ALU.add).then_inc(c.step(), 1)
                e.wait_ge(c.sem, c.last())
                STT(codes, base4, float(CAP), rank4, ALU.mult, ALU.add).then_inc(c.step(), 1)

                def extra_units():
                    TS(fg4, thr_grp[0:1, :], upto[0:1, NE - 1:NE], None, ALU.is_lt).then_inc(c.step(), 1)
                    TT(later, upto[0:1, :].unsqueeze(1).to_broadcast([1, MAXX, NE]),
                       iota[0:1, 0:MAXX].unsqueeze(2).to_broadcast([1, MAXX, NE]), ALU.is_le).then_inc(c.step(), 1)
                    e.wait_ge(c.sem, c.last())
                    V.tensor_reduce(fgrp[0:1, 0:1], fg4, AX, ALU.add).then_inc(c.step(), 1)
                    V.tensor_reduce(xe, later, AX, ALU.add).then_inc(c.step(), 1)
                    e.wait_ge(c.sem, c.last())
                    V.tensor_copy(xinfo[0:1, ds(l, 1), 0:1], fgrp[0:1, 0:1].unsqueeze(1)).then_inc(c.step(), 1)
                    V.tensor_copy(xinfo[0:1, ds(l, 1), 1:2], xsum[0:1, :].unsqueeze(1)).then_inc(c.step(), 1)
                    TS(xinfo[0:1, ds(l, 1), 2:2 + MAXX], xe.unsqueeze(1), float(NE - 1), None, ALU.min).then_inc(c.step(), 1)
                    e.wait_ge(c.sem, c.last())
                    TT(xsum[0:1, :], xsum[0:1, :], fgrp[0:1, 0:1], ALU.add).then_inc(routed.sem, 1)

                e.wait_ge(c.sem, c.last())
                experts(main, l * GROUPS, extra_units)
                c.end()
                with e.Fori(1, GROUPS) as g:
                    experts(main, l * GROUPS + g)
                count, prior = extra_groups(e, l)
                with e.If(count > 0):
                    with e.Fori(0, count) as t:
                        experts(extra, prior + t)
                layer_sums(e, l, count, prior)


INS = ["x", "positions", "norm_mix_g", "w_in", "attn_q_norm_g", "attn_k_norm_g", "lambda_q1", "lambda_k1",
       "lambda_q2", "lambda_k2", "attn_subln_g", "hgrn_lower_bounds", "hgrn_norm_g", "conv_w", "w_out",
       "norm_ffn_g", "router_group_w", "router_group_b", "router_expert_w", "router_expert_b",
       "expert_w_gate", "expert_w_up", "expert_w_down"]


def kernel(**inputs):
    import numpy as _np
    import concourse.bacc as _bacc
    from concourse import mybir as _mybir
    from concourse.bass_utils import run_bass_kernel_spmd as _run

    nc = _bacc.Bacc("TRN2", target_bir_lowering=False, num_devices=1)
    arrays, aps = {}, {}
    for name in INS:
        v = _np.ascontiguousarray(inputs[name])
        arrays[f"in_{name}"] = v
        aps[name] = nc.dram_tensor(f"in_{name}", v.shape, _mybir.dt.from_np(v.dtype), kind="ExternalInput").ap()
    shape = arrays["in_x"].shape
    out = nc.dram_tensor("out", shape, _mybir.dt.float32, kind="ExternalOutput").ap()
    hybrid_trunk(nc, aps, out)
    r = _run(nc, [arrays], core_ids=[0])
    return r.results[0]["out"]
```

```python
import math
from contextlib import ExitStack

import numpy as np
import concourse.bass as bass
from concourse import mybir

F32 = mybir.dt.float32
I32 = mybir.dt.int32
U32 = mybir.dt.uint32
ALU = mybir.AluOpType
ACT = mybir.ActivationFunctionType
AX = mybir.AxisListType.X
ds = bass.ds

P = 128

CONSTS = 47
IDENT_MADE = 13
DVE_M = 226
DVE_G = 20
POOL_M = 2


class Signal:

    def __init__(self, sem, per, credit=0):
        self.sem, self.per, self.credit = sem, per, credit

    def after(self, turn, n):
        return turn * self.per + (n + self.credit)


class Chain:

    def __init__(self, signal, turn):
        self.own, self.turn, self.sem, self.n = signal, turn, signal.sem, 0

    def step(self):
        self.n += 1
        return self.sem

    def last(self):
        return self.own.after(self.turn, self.n)

    def end(self):
        assert self.n == self.own.per, (self.sem, self.n, self.own.per)


def hybrid_trunk(nc, a, out):
    DEPTH, D = a["norm_mix_g"].shape
    SEQ = a["x"].shape[1]
    D_IN = a["w_in"].shape[2]
    TI = SEQ // P
    KT = D // P
    DK = a["attn_q_norm_g"].shape[1]
    DV = a["attn_subln_g"].shape[1]
    HA = 4
    HC = 2 * HA
    HALF = DK // 8
    DB = a["hgrn_norm_g"].shape[1]
    HB = 4
    HP = HB * DB // P
    CW = a["conv_w"].shape[2]
    NG = a["router_group_w"].shape[2]
    NE = a["router_expert_w"].shape[2]
    EPG = NE // NG
    DE = a["expert_w_gate"].shape[3]
    CHUNK = 64
    EPS, TINY, MASKED = 1e-6, 1e-30, -1e30
    NK = 2
    CAP = 32
    UG = 4
    GROUPS = NE // UG
    MAXX = SEQ * NK // CAP
    R = 6
    AHEAD, IN_MAPS, IN_WORK, IN_HT = R, R + 1, R + 2, R + 3
    SLOT = 4096
    NO_SLOT = 65536.0
    LN_CUT = 2.0 ** -60
    assert TI == 2 and KT == 8 and HP == 2 and CW == 2 * P and DE == 4 * P

    ctx = ExitStack()
    with ctx:
        def sb(name, shape, dt=F32):
            return ctx.enter_context(nc.sbuf_tensor(name, shape, dt))

        def sig(name, per, credit=0):
            return Signal(ctx.enter_context(nc.semaphore(name)), per, credit)

        ring = sb("ring", [P, R + 1, SLOT])
        x = sb("x", [P, TI, D])
        h = sb("h", [P, TI, KT, P])
        hT = sb("hT", [P, KT, SEQ])
        mixT = hT
        ident = sb("ident", [P, P])
        before = sb("before", [P, P])
        ones = sb("ones", [P, P])
        iota = sb("iota", [P, P])
        LEVELS = [0, 64, 32, 16, 8, 4, 2, 1]
        masks = sb("masks", [P, len(LEVELS), P])
        restart = sb("restart", [P, HP, SEQ])
        attn_mask = sb("attn_mask", [P, CHUNK])
        cosb = sb("cosb", [P, TI, HALF])
        sinb = sb("sinb", [P, TI, HALF])
        table = sb("table", [P, DEPTH, 11])
        cur = sb("cur", [P, 11])
        prow = sb("prow", [DEPTH * 8, P])
        pcol = sb("pcol", [P, DEPTH * 8])
        pos_i = sb("pos_i", [P, TI], I32)
        small = sb("small", [P, 512])
        gmix = sb("gmix", [P, KT])
        gffn = sb("gffn", [P, KT])
        gffn_in = sb("gffn_in", [P, KT])
        wr = sb("wr", [P, KT, NG + NE])
        qkg = sb("qkg", [P, 2, DK])
        subg = sb("subg", [P, DV])
        hng = sb("hng", [P, DB])
        rb = sb("rb", [P, NG + NE])
        lamv = sb("lamv", [P, 4, DK])
        xinfo = sb("xinfo", [1, DEPTH, 2 + MAXX], I32)
        work = sb("work", [P, 19, 512])
        hg = work[:, 0:6, :]
        u = work[:, 6:19, :]
        maps = sb("maps", [P, 2 * HC, SEQ])
        qkT = maps[:, 0:HC, :]
        sm = maps[:, HC:2 * HC, :]
        sT = h[:, 0, :, :].rearrange("p (a m) t -> p a m t", a=2)
        far = h[:, 1, 0:2 * HP, :].rearrange("p (a m) t -> p a m t", a=2)

        apart = [u[:, n, :].rearrange("p (m a t) -> p m a t", a=2, t=P // 2) for n in range(2)]
        G_, Q_, KEY_, D_, Z0_ = 0, 1, 2, 3, 4
        oa_junk = h[:, 1, 4:8, :]
        ob_junk = hg[:, Z0_ + 1, :].rearrange("p (m d) -> p m d", d=DB)
        x_junk = u[:, 2:4, :].rearrange("p a n -> p (a n)")
        wT = hg[:, 0:3, :].rearrange("p a (n k) -> p (a n) k", k=P)
        bq, bf, aq, cbT, ccT, cxT = u[:, 0, :], u[:, 1, :], u[:, 2:6, :], u[:, 10, :], u[:, 11, :], u[:, 12, :]
        av = u[:, 6:8, :]
        bib = u[:, 8:10, :]
        qk = aq.rearrange("p (j i) n -> p j i n", j=2)
        att_w = u[:, 2:4, :].rearrange("p a n -> p (a n)").rearrange("p (h k) -> p h k", h=HA)
        oa = u[:, 4:6, :]
        ob = hg[:, Z0_, :]
        egate = hg[:, D_, :]
        xg = u[:, 2:4, :].rearrange("p a (k c) -> p (a k) c", c=P)
        ye = u[:, 4:6, :].rearrange("p a n -> p (a n)")
        sel = u[:, 6, 0:TI * P].rearrange("p (i c) -> p i c", i=TI)
        gat = u[:, 6, TI * P:2 * TI * P].rearrange("p (i c) -> p i c", i=TI)
        gtmp = u[:, 7, 0:TI * P].rearrange("p (i c) -> p i c", i=TI)
        gatT = u[:, 7, TI * P:2 * TI * P]
        sil, silr, actv = ([u[:, b, n * P:n * P + P] for b in (8, 12)] for n in range(3))
        actT = u[:, 8, 3 * P:4 * P]
        smf = sm[:, :, :].rearrange("p m n -> p (m n)")
        rt, rt2, rt3 = u[:, 9, :], u[:, 10, :], u[:, 11, :]
        lg = rt[:, 0:TI * 40].rearrange("p (i n) -> p i n", i=TI)
        mg = rt[:, 80:96].rearrange("p (i n) -> p i n", i=TI)
        nmg, gidx, edif = rt[:, 96:98], rt[:, 98:100], rt[:, 196:198]
        ohg = rt[:, 100:108].rearrange("p (i n) -> p i n", i=TI)
        pen = rt[:, 108:116].rearrange("p (i n) -> p i n", i=TI)
        em = rt[:, 116:180].rearrange("p (i n) -> p i n", i=TI)
        mv = rt[:, 180:196].rearrange("p (i n) -> p i n", i=TI)
        eidf = rt[:, 198:202]
        eid = eidf.rearrange("p (k i) -> p k i", k=NK)
        rjunk = rt[:, 202:210].rearrange("p (i n) -> p i n", i=TI)
        picks = rt[:, 256:256 + TI * NE].rearrange("p (i n) -> p i n", i=TI)
        oh = rt[:, 320:320 + NK * TI * NE].rearrange("p (m n) -> p m n", n=NE)
        units, upto = rt[:, 448:448 + NE], rt[:, 480:480 + NE]
        prod4 = rt2[:, 0:NK * TI * NE].rearrange("p (m n) -> p m n", n=NE)
        over = rt2[:, 128:128 + NE * (SEQ // CAP - 1)].rearrange("p (n m) -> p n m", n=NE)
        base4, rank4, full4, fg4, xe = rt2[:, 384:388], rt2[:, 388:392], rt2[:, 392:396], rt2[0:1, 396:400], rt2[0:1, 400:416]
        counts = rt2[:, 416:416 + NE]
        later = rt3[0:1, 0:MAXX * NE].rearrange("p (m n) -> p m n", n=NE)
        idx = sb("idx", [P, 2 * TI, 8], U32)

        def col(a0, n):
            return small[:, a0:a0 + n]

        ssq, rstd = col(0, 2), col(4, 2)
        qk_ms, qk_rs = col(8, 16), col(24, 16)
        negmax, denom, inv = col(40, 16), col(56, 16), col(72, 16)
        oa_ms, oa_rs = col(88, 8), col(96, 8)
        ob_ms, ob_rs = col(104, 8), col(112, 8)
        lam_s, lam_e, nlam, subs = col(120, 2), col(122, 2), col(124, 1), col(125, 1)
        codes, gates = col(128, 4), col(132, 4)
        xcodes = col(304, 4)
        xsum = col(136, 1)
        fgrp = col(140, 4)
        thr_cap = col(144, SEQ // CAP - 1)
        thr_grp = col(152, MAXX // UG)
        pos_f, ang = col(160, 2), col(168, TI * HALF)
        turn_n, angc = col(184, TI * HALF), col(200, TI * HALF)
        freq = col(216, HALF)
        lbt = col(224, DEPTH * HP)
        lbm = col(232, HP)
        lbs = col(236, HP)
        eps = col(240, 1)
        expsum = col(248, 2)
        warm = col(250, 1)
        rs_v, rs_h, rs_w = col(256, 16), col(272, 16), col(288, 16)
        subgl = sb("subgl", [P, DV])

        bank = [ctx.enter_context(nc.psum_tensor(f"bank{i}", [P, 512], F32)) for i in range(8)]

        c_aq, c_ak, c_av, c_bq, c_bi, c_cb, c_cx = 0, 512, 1024, 1536, 2048, 2560, 3072
        assert c_cx + CW == D_IN
        SECTIONS = [(c_bq, 512, 3), (c_aq, 512, 4), (c_ak, 512, 5), (c_av, 512, 0), (c_bi, 512, 1), (c_cb, 512, 2),
                    (c_cx, 256, 0)]
        WOUT = (1, 2)

        def slots_of(i):
            return (3, 4, 5) if i % 2 == 0 else (0, 1, 2)

        FIRST = [(3, 4, 5), (0, AHEAD, IN_MAPS), (1, 2, IN_WORK), (0, AHEAD, IN_MAPS)]

        def slot(s):
            if s == IN_MAPS:
                return maps[:, :, :].rearrange("p m n -> p (m n)")
            if s == IN_WORK:
                return work[:, 0:8, :].rearrange("p m n -> p (m n)")
            return ring[:, s, :]

        def down_tiles(s, half_in_ht=False):
            tiles = slot(s).rearrange("p (j n) -> p j n", j=4)
            early = hT[:, :, :].rearrange("p (j k) t -> p j (k t)", j=2)
            return [(early if half_in_ht and j < 2 else tiles)[:, j, :] for j in range(4)]

        def loads(s, i):
            if s == IN_HT:
                return 1
            before = sum(s == at for _, _, at in SECTIONS) + sum(s == at for at in WOUT)
            return before + sum(s in FIRST[at] for at in range(i + 1))

        x_in, pos_in, rows_in, out_done = sig("x_in", 0), sig("pos_in", 0), sig("rows_in", 0), sig("out_done", 0)
        const_ok = sig("const_ok", CONSTS)
        settled = sig("settled", 0)
        stream_ok = sig("stream_ok", 1)
        dve_p = sig("dve_p", 0)
        pro_dve, pro_act, pro_pe = sig("pro_dve", 0), sig("pro_act", 0), sig("pro_pe", 0)
        params_in, router_in = sig("params_in", 16 * 10), sig("router_in", 16 * 4)
        ring_full = [sig(f"ring_full{s}", 16 * (loads(s, UG - 1) + (2 * (GROUPS - 1) if s < R else 0)))
                     for s in range(R + 4)]
        xring_full = [sig(f"xring_full{i}", 32) for i in range(R)]
        dve_m = sig("dve_m", DVE_M)
        sums_ok, h_ok, ht_ps, ht_sb = sig("sums_ok", 4), sig("h_ok", 4), sig("ht_ps", 8), sig("ht_sb", 8)
        proj_ps, proj_sb = sig("proj_ps", 13), sig("proj_sb", 13)
        hg_dve, hg_act, hg_qk = sig("hg_dve", 2), sig("hg_act", 3), sig("hg_qk", 1)
        z_diff, z_exp, z_ok = sig("z_diff", 8), sig("z_exp", 8), sig("z_ok", 8)
        lev_ps, lev_sb = sig("lev_ps", 9), sig("lev_sb", 9)
        qk_sq, qk_ok = sig("qk_sq", 2), sig("qk_ok", 2)
        qkt_ps, qkt_sb = sig("qkt_ps", 4), sig("qkt_sb", 4)
        sc_ps, max_ok, exp_ok, w_ok = sig("sc_ps", 2), sig("max_ok", 2), sig("exp_ok", 2), sig("w_ok", 2)
        wt_ps, wt_sb, pv_ps = sig("wt_ps", 3), sig("wt_sb", 3), sig("pv_ps", 2)
        oa_sq, oa_ok, oat_ps, oat_sb = sig("oa_sq", 2), sig("oa_ok", 2), sig("oat_ps", 2), sig("oat_sb", 2)
        gate_sum, gate_rec, gate_ok = sig("gate_sum", 1), sig("gate_rec", 1), sig("gate_ok", 1)
        gate_exp, ob_ps, ob_sq = sig("gate_exp", 1), sig("ob_ps", 1), sig("ob_sq", 1)
        ob_ok, obt_ps, obt_sb = sig("ob_ok", 1), sig("obt_ps", 1), sig("obt_sb", 1)
        pool_m = sig("pool_m", POOL_M)
        conv_in, taps_ok = sig("conv_in", 1), sig("taps_ok", 1)
        conv_ok, lam_sum, lam_exp = sig("conv_ok", 1), sig("lam_sum", 1), sig("lam_exp", 1)
        op_ps, x_mixed = sig("op_ps", 4), sig("x_mixed", 4)
        log_ps, top_g, exp_g = sig("log_ps", 1), sig("top_g", 1), sig("exp_g", 1)
        top_e, exp_e, picks_ok = sig("top_e", 1), sig("exp_e", 1), sig("picks_ok", 1)
        rank_ps, routed = sig("rank_ps", 1), sig("routed", 1)

        class Experts:

            def __init__(self, t, full):
                self.dve = sig(t + "dve", DVE_G, 1)
                self.gat_ok = sig(t + "gat_ok", 1)
                self.sel_ok, self.gath_ps, self.xg_ok = sig(t + "sel_ok", 1), sig(t + "gath_ps", 2), sig(t + "xg_ok", 2)
                self.gat_ps, self.gat_sb = sig(t + "gat_ps", 1), sig(t + "gat_sb", 1)
                self.gu_ps, self.gu_exp, self.act_ok = sig(t + "gu_ps", 4, 2), sig(t + "gu_exp", 4), sig(t + "act_ok", 4)
                self.at_ps, self.at_sb = sig(t + "at_ps", 4), sig(t + "at_sb", 4)
                self.ye_ps, self.ye_act, self.ye_dve = sig(t + "ye_ps", 4, 2), sig(t + "ye_act", 4), sig(t + "ye_dve", 4)
                self.scat_ps, self.x_added = sig(t + "scat_ps", 4), sig(t + "x_added", 4, 1)
                self.full = full

        main = Experts("m_", ring_full)
        extra = Experts("x_", xring_full)

        block = ctx.enter_context(nc.Block())

        IN_TURN = [(part, i) for i in range(UG) for part in ("up", "down")]
        OVERLAPPED = [("up", 0), ("up", 1), ("down", 0), ("up", 2), ("down", 1), ("up", 3), ("down", 2), ("down", 3)]
        GU_BANK = (4, 6)

        def settle(e):
            e.sem_inc(settled.sem, 1)

        def extra_groups(e, l):
            e.wait_ge(routed.sem, routed.after(l, 1))
            settle(e)
            count = e.value_load(xinfo[0:1, ds(l, 1), 0:1], min_val=0, max_val=MAXX // UG)
            prior = e.value_load(xinfo[0:1, ds(l, 1), 1:2], min_val=0, max_val=DEPTH * MAXX // UG)
            return count, prior

        def layer_sums(e, l, count, prior):
            e.wait_ge(main.x_added.sem, main.x_added.after(l * GROUPS + GROUPS, 0))
            e.wait_ge(extra.x_added.sem, extra.x_added.after(prior + count, 0))

        def row(name, l):
            return a[name][ds(l, 1)].to_broadcast([P, a[name].shape[1]])

        def mixer_parameters(e, l):
            for dst, src in (
                    (gmix[:, :], a["norm_mix_g"][ds(l, 1)].rearrange("l (p k) -> p (l k)", k=KT)),
                    (lamv[:, 0, :], row("lambda_q1", l)), (lamv[:, 1, :], row("lambda_k1", l)),
                    (lamv[:, 2, :], row("lambda_q2", l)), (lamv[:, 3, :], row("lambda_k2", l)),
                    (gffn_in[:, :], a["norm_ffn_g"][ds(l, 1)].rearrange("l (p k) -> p (l k)", k=KT)),
                    (qkg[:, 0, :], row("attn_q_norm_g", l)), (qkg[:, 1, :], row("attn_k_norm_g", l)),
                    (subg[:, :], row("attn_subln_g", l)), (hng[:, :], row("hgrn_norm_g", l))):
                e.dma_start(dst, src).then_inc(params_in.sem, 16)

        def router_parameters(e, l):
            for dst, src in (
                    (rb[:, NE:NE + NG], row("router_group_b", l)), (rb[:, 0:NE], row("router_expert_b", l)),
                    (wr[:, :, NE:NE + NG], a["router_group_w"][ds(l, 1)].rearrange("l (p k) n -> p (l k) n", k=KT)),
                    (wr[:, :, 0:NE], a["router_expert_w"][ds(l, 1)].rearrange("l (p k) n -> p (l k) n", k=KT))):
                e.dma_start(dst, src).then_inc(router_in.sem, 16)

        @block.sync
        def _(e):
            e.dma_start(prow[0:DEPTH * HP, :], a["hgrn_lower_bounds"].rearrange("l (h p) -> (l h) p", p=P)).then_inc(rows_in.sem, 16)
            e.dma_start(prow[DEPTH * HP:DEPTH * 8, :], a["conv_w"].rearrange("l j (c p) -> (l j c) p", p=P)).then_inc(rows_in.sem, 16)
            e.dma_start(pos_i[:, :], a["positions"][0].rearrange("(i p) -> p i", p=P),
                        allow_slow_non_contiguous=True).then_inc(pos_in.sem, 16)
            e.dma_start(x[:, :, :], a["x"][0].rearrange("(i p) d -> p i d", p=P)).then_inc(x_in.sem, 16)
            mixer_parameters(e, 0)
            router_parameters(e, 0)
            with e.Fori(0, DEPTH) as l:
                w_in = a["w_in"][ds(l, 1)].rearrange("l (p k) n -> p (l k) n", k=KT)
                w_out = a["w_out"][ds(l, 1)].rearrange("l (k p) n -> p (l k) n", k=KT)

                def section(n):
                    c0, width, s = SECTIONS[n]
                    e.dma_start(ring[:, s, 0:KT * width].rearrange("p (k n) -> p k n", k=KT),
                                w_in[:, :, c0:c0 + width]).then_inc(ring_full[s].sem, 16)

                def part(full, s, ex, n):
                    if n < 2:
                        src = a[("expert_w_gate", "expert_w_up")[n]][ds(l, 1), ds(ex, 1)].rearrange("l e (p k) n -> p (l e k n)", k=KT)
                        e.dma_start(slot(s), src).then_inc(full[s].sem, 16)
                    else:
                        src = a["expert_w_down"][ds(l, 1), ds(ex, 1)].rearrange("l e (j p) n -> p (l e j) n", p=P)
                        e.dma_start(slot(s).rearrange("p (j n) -> p j n", j=4), src).then_inc(full[s].sem, 16)

                def half_down(dst, s, ex, half):
                    src = a["expert_w_down"][ds(l, 1), ds(ex, 1)].rearrange("l e (j p) n -> p (l e j) n", p=P)
                    e.dma_start(dst, src[:, 2 * half:2 * half + 2, :]).then_inc(ring_full[s].sem, 16)

                def unit(full, S, turn, i, ex):
                    sg, su, sd = slots_of(i)
                    e.wait_ge(S.gu_ps.sem, S.gu_ps.after(turn, i - 1))
                    part(full, sg, ex, 0)
                    part(full, su, ex, 1)
                    e.wait_ge(S.ye_ps.sem, S.ye_ps.after(turn, i - 1))
                    part(full, sd, ex, 2)

                first = l * GROUPS
                e.wait_ge(main.gu_ps.sem, main.gu_ps.after(first, -1))
                section(0)
                section(1)
                e.wait_ge(main.ye_ps.sem, main.ye_ps.after(first, -1))
                section(2)
                e.wait_ge(main.gu_ps.sem, main.gu_ps.after(first, 0))
                section(3)
                section(4)
                e.wait_ge(main.ye_ps.sem, main.ye_ps.after(first, 0))
                section(5)
                for n in range(3):
                    e.wait_ge(proj_ps.sem, proj_ps.after(l, 2 * n + 2))
                    part(ring_full, FIRST[0][n], 0, n)
                e.wait_ge(proj_ps.sem, proj_ps.after(l, 8))
                section(6)
                for n in range(2):
                    e.wait_ge(proj_ps.sem, proj_ps.after(l, 10 + 2 * n))
                    e.dma_start(ring[:, WOUT[n], :].rearrange("p (k n) -> p k n", k=KT),
                                w_out[:, :, n * 512:n * 512 + 512]).then_inc(ring_full[WOUT[n]].sem, 16)
                e.wait_ge(proj_ps.sem, proj_ps.after(l, 13))
                part(ring_full, FIRST[1][0], 1, 0)
                part(ring_full, FIRST[1][1], 1, 1)
                e.wait_ge(w_ok.sem, w_ok.after(l, 2))
                part(ring_full, FIRST[1][2], 1, 2)
                e.wait_ge(obt_ps.sem, obt_ps.after(l, 1))
                part(ring_full, FIRST[2][2], 2, 2)
                e.wait_ge(op_ps.sem, op_ps.after(l, 4))
                part(ring_full, FIRST[2][0], 2, 0)
                part(ring_full, FIRST[2][1], 2, 1)
                e.wait_ge(log_ps.sem, log_ps.after(l, 1))
                half_down(hT[:, :, :].rearrange("p (j k) t -> p j (k t)", j=2), IN_HT, 3, 0)
                e.wait_ge(main.gu_ps.sem, main.gu_ps.after(first, 1))
                part(ring_full, slots_of(4)[0], 4, 0)
                part(ring_full, slots_of(4)[1], 4, 1)
                e.wait_ge(main.gu_ps.sem, main.gu_ps.after(first, 2))
                part(ring_full, FIRST[3][0], 3, 0)
                part(ring_full, FIRST[3][1], 3, 1)
                e.wait_ge(main.ye_ps.sem, main.ye_ps.after(first, 2))
                half_down(slot(IN_MAPS).rearrange("p (j n) -> p j n", j=4)[:, 2:4, :], IN_MAPS, 3, 1)
                part(ring_full, slots_of(4)[2], 4, 2)
                for i in range(1, UG):
                    unit(ring_full, main, first + 1, i, UG + i)
                with e.Fori(2, GROUPS) as g:
                    for i in range(UG):
                        unit(ring_full, main, l * GROUPS + g, i, g * UG + i)
                count, prior = extra_groups(e, l)
                with e.If(count > 0):
                    with e.Fori(0, count) as t:
                        e.wait_ge(main.x_added.sem, main.x_added.after(l * GROUPS + GROUPS, 0))
                        for i in range(UG):
                            ex = e.value_load(xinfo[0:1, ds(l, 1), ds(t * UG + (2 + i), 1)], min_val=0, max_val=NE - 1)
                            unit(xring_full, extra, prior + t, i, ex)
                        e.wait_ge(extra.x_added.sem, extra.x_added.after(prior + t, 4))
                        settle(e)
            count, prior = extra_groups(e, DEPTH - 1)
            layer_sums(e, DEPTH - 1, count, prior)
            e.dma_start(out[0].rearrange("(i p) d -> p i d", p=P), x[:, :, :]).then_inc(out_done.sem, 16)
            e.wait_ge(out_done.sem, 16)

        @block.gpsimd
        def _(e):
            def gates_and_convolution(e, l):
                c = Chain(pool_m, l)
                G = nc.gpsimd
                e.wait_ge(gate_exp.sem, gate_exp.after(l, 1))
                settle(e)
                G.tensor_scalar(egate, egate, 1.0, None, ALU.add).then_inc(gate_sum.sem, 1)
                e.wait_ge(gate_rec.sem, gate_rec.after(l, 1))
                gview = egate.rearrange("p (i n) -> p i n", i=TI)
                G.tensor_tensor(gview, gview, bib[:, :, HB * DB:2 * HB * DB], ALU.mult).then_inc(gate_ok.sem, 1)
                e.wait_ge(proj_sb.sem, proj_sb.after(l, 13))
                G.tensor_tensor(ccT, ccT, cxT, ALU.mult).then_inc(conv_in.sem, 1)
                e.wait_ge(taps_ok.sem, taps_ok.after(l, 1))
                for back, tap in ((1, bq), (2, bf)):
                    y, t = (v.rearrange("p (c t) -> p c t", c=2) for v in (cxT, tap))
                    G.tensor_tensor(y[:, :, back:SEQ], y[:, :, back:SEQ], t[:, :, 0:SEQ - back], ALU.add).then_inc(c.step(), 1)
                    e.wait_ge(c.sem, c.last())
                G.tensor_tensor(mixT[:, 6:8, :], cxT.rearrange("p (c t) -> p c t", c=2),
                                cbT.rearrange("p (c t) -> p c t", c=2), ALU.mult).then_inc(conv_ok.sem, 1)
                c.end()

            made = Chain(const_ok, 0)

            nc.gpsimd.memset(ident[:, :], 0.0).then_inc(made.step(), 1)
            nc.gpsimd.memset(before[:, :], 1.0).then_inc(made.step(), 1)
            nc.gpsimd.memset(ones[:, :], 1.0).then_inc(made.step(), 1)
            nc.gpsimd.memset(eps, EPS).then_inc(made.step(), 1)
            inv_freq = np.float32(500000.0) ** (-np.arange(0, 2 * HALF, 2, dtype=np.float32) / np.float32(2 * HALF))
            for n in range(HALF):
                nc.gpsimd.memset(freq[:, n:n + 1], float(inv_freq[n])).then_inc(made.step(), 1)
            e.wait_ge(made.sem, made.last())
            nc.gpsimd.affine_select(out=ident[:, :], in_=ident[:, :], compare_op=ALU.not_equal, fill=1.0,
                                    base=0, pattern=[[-1, P]], channel_multiplier=1).then_inc(made.step(), 1)
            assert made.last() == IDENT_MADE, made.last()
            nc.gpsimd.affine_select(out=before[:, :], in_=before[:, :], compare_op=ALU.is_gt, fill=0.0,
                                    base=0, pattern=[[1, P]], channel_multiplier=-1).then_inc(made.step(), 1)
            nc.gpsimd.iota(iota[:, :], [[1, P]], base=0, channel_multiplier=0, allow_small_or_imprecise_dtypes=True).then_inc(made.step(), 1)
            nc.gpsimd.iota(thr_cap, [[CAP, SEQ // CAP - 1]], base=CAP, channel_multiplier=0, allow_small_or_imprecise_dtypes=True).then_inc(made.step(), 1)
            nc.gpsimd.iota(thr_grp, [[UG, MAXX // UG]], base=0, channel_multiplier=0, allow_small_or_imprecise_dtypes=True).then_inc(made.step(), 1)
            nc.gpsimd.memset(xsum, 0.0).then_inc(made.step(), 1)
            for n in range(DEPTH):
                nc.gpsimd.memset(table[:, n, 10:11], 0.8 - 0.6 * math.exp(-0.3 * n)).then_inc(made.step(), 1)
            nc.gpsimd.memset(restart[:, :, :], 1.0).then_inc(made.step(), 1)
            nc.gpsimd.memset(masks[:, :, :], 0.0).then_inc(made.step(), 1)
            nc.gpsimd.memset(attn_mask[:, :], MASKED).then_inc(made.step(), 1)
            e.wait_ge(made.sem, made.last())
            nc.gpsimd.affine_select(out=attn_mask[:, :], in_=attn_mask[:, :], compare_op=ALU.is_ge, fill=0.0,
                                    base=CHUNK - 1, pattern=[[0, CHUNK]], channel_multiplier=-1).then_inc(made.step(), 1)
            nc.gpsimd.memset(restart[:, :, :].rearrange("p h (c t) -> p (h c) t", t=CHUNK)[:, :, 0:1], 0.0).then_inc(made.step(), 1)
            nc.gpsimd.affine_select(out=masks[:, 0, :], in_=masks[:, 0, :], compare_op=ALU.not_equal, fill=1.0,
                                    base=0, pattern=[[-1, P]], channel_multiplier=1).then_inc(made.step(), 1)

            def second_blocks(n, B):
                return masks[:, n, :].rearrange("p (b o t) -> p b o t", o=2, t=B)[:, :, 1, :]

            for n, B in enumerate(LEVELS[1:], 1):
                nc.gpsimd.memset(second_blocks(n, B), 1.0).then_inc(made.step(), 1)
            e.wait_ge(made.sem, made.last())
            for n, B in enumerate(LEVELS[1:], 1):
                v = second_blocks(n, B)
                nc.gpsimd.affine_select(out=v, in_=v, compare_op=ALU.is_ge, fill=0.0, base=0,
                                        pattern=[[-2 * B, P // (2 * B)], [0, B]], channel_multiplier=1).then_inc(made.step(), 1)
            e.wait_ge(made.sem, made.last())
            for n, B in enumerate(LEVELS[1:], 1):
                v = second_blocks(n, B)
                nc.gpsimd.affine_select(out=v, in_=v, compare_op=ALU.is_ge, fill=0.0, base=B - 1,
                                        pattern=[[2 * B, P // (2 * B)], [0, B]], channel_multiplier=-1).then_inc(made.step(), 1)
            made.end()
            with e.Fori(0, DEPTH) as l:
                gates_and_convolution(e, l)

        @block.tensor
        def _(e):
            T = nc.tensor
            for S in (main, extra):
                e.sem_inc(S.gu_ps.sem, 2)
                e.sem_inc(S.ye_ps.sem, 2)
            e.wait_ge(const_ok.sem, IDENT_MADE)
            e.wait_ge(rows_in.sem, 32)
            T.transpose(bank[0][:, 0:DEPTH * 8], prow[:, :], ident[0:DEPTH * 8, 0:DEPTH * 8]).then_inc(pro_pe.sem, 1)
            e.wait_ge(pro_dve.sem, 1)
            e.wait_ge(const_ok.sem, CONSTS)

            def transposed_rows(i, rows):
                for half in range(2):
                    for k in range(4):
                        last = T.transpose(bank[2 * i + half][:, k * P:k * P + P], rows[:, 4 * half + k, :], ident[:, :])
                    last.then_inc(ht_ps.sem, 1)

            def experts(S, turn, order, slots_of, loaded):
                e.wait_ge(S.sel_ok.sem, S.sel_ok.after(turn, 1))
                for half in range(2):
                    for k in range(4):
                        for i in range(TI):
                            last = T.matmul(bank[half][:, k * P:k * P + P], h[:, i, 4 * half + k, :], sel[:, i, :],
                                            start=(i == 0), stop=(i == TI - 1))
                    last.then_inc(S.gath_ps.sem, 1)
                e.wait_ge(S.gat_ok.sem, S.gat_ok.after(turn, 1))
                for i in range(TI):
                    last = T.transpose(bank[2][:, i * P:i * P + P], gat[:, i, :], ident[:, :])
                last.then_inc(S.gat_ps.sem, 1)
                for part, i in order:
                    sg, su, sd = slots_of(i)
                    if part == "up":
                        e.wait_ge(S.full[sg].sem, loaded(sg, i))
                        e.wait_ge(S.full[su].sem, loaded(su, i))
                        gate_up = ring[:, sg:su + 1:su - sg, :].rearrange("p a (k n) -> p a k n", k=KT)
                        for k in range(KT):
                            if i == 0 and k % 4 == 0:
                                e.wait_ge(S.xg_ok.sem, S.xg_ok.after(turn, 1 + k // 4))
                            for j in range(4):
                                last = T.matmul(bank[GU_BANK[i % 2]][CAP * j:CAP * j + CAP, 0:2 * P], xg[:, k, CAP * i:CAP * i + CAP],
                                                gate_up[:, :, k, P * j:P * j + P], start=(k == 0), stop=(k == KT - 1))
                        last.then_inc(S.gu_ps.sem, 1)
                        continue
                    e.wait_ge(S.act_ok.sem, S.act_ok.after(turn, i + 1))
                    T.transpose(bank[3][:, 0:P], actv[i % 2], ident[:, :]).then_inc(S.at_ps.sem, 1)
                    if i:
                        e.wait_ge(S.ye_act.sem, S.ye_act.after(turn, i))
                        e.wait_ge(S.ye_dve.sem, S.ye_dve.after(turn, i))
                    e.wait_ge(S.full[sd].sem, loaded(sd, i))
                    e.wait_ge(S.at_sb.sem, S.at_sb.after(turn, i + 1))
                    early = order is OVERLAPPED and i == UG - 1
                    if early:
                        e.wait_ge(S.full[IN_HT].sem, loaded(IN_HT, i))
                    down = down_tiles(sd, early)
                    for j in range(4):
                        for q in range(4):
                            last = T.matmul(bank[5][CAP * q:CAP * q + CAP, 0:2 * P], actT[:, CAP * j:CAP * j + CAP],
                                            down[j][:, 2 * P * q:2 * P * q + 2 * P], start=(j == 0), stop=(j == 3))
                    last.then_inc(S.ye_ps.sem, 1)
                e.wait_ge(S.gat_sb.sem, S.gat_sb.after(turn, 1))
                e.wait_ge(S.ye_act.sem, S.ye_act.after(turn, 4))
                e.wait_ge(S.ye_dve.sem, S.ye_dve.after(turn, 4))
                for n in range(4):
                    i, half = n // 2, n % 2
                    T.matmul(bank[(6, 7, 0, 1)[n]][:, :], gatT[:, i * P:i * P + P], ye[:, half * 512:half * 512 + 512],
                             start=True, stop=True).then_inc(S.scat_ps.sem, 1)

            with e.Fori(0, DEPTH) as l:
                for i in range(TI):
                    e.wait_ge(h_ok.sem, h_ok.after(l, i + 1))
                    transposed_rows(i, h[:, i, :, :])

                def section(n):
                    c0, width, s = SECTIONS[n]
                    e.wait_ge(ring_full[s].sem, ring_full[s].after(l, 32 if n == 6 else 16))
                    return ring[:, s, 0:KT * width].rearrange("p (k n) -> p k n", k=KT)

                def project_rows(W, b, i):
                    for k in range(KT):
                        last = T.matmul(bank[b][:, :], hT[:, k, i * P:i * P + P], W[:, k, :],
                                        start=(k == 0), stop=(k == KT - 1))
                    last.then_inc(proj_ps.sem, 1)

                def project_columns(W, b, pair):
                    for c in range(2):
                        for k in range(KT):
                            c0 = pair * 256 + c * P
                            last = T.matmul(bank[b][:, c * SEQ:c * SEQ + SEQ], W[:, k, c0:c0 + P], hT[:, k, :],
                                            start=(k == 0), stop=(k == KT - 1))
                    last.then_inc(proj_ps.sem, 1)

                def proj_read(n):
                    e.wait_ge(proj_sb.sem, proj_sb.after(l, n))

                def level(n):
                    if n == 0:
                        e.wait_ge(hg_qk.sem, hg_qk.after(l, 1))
                        left, right = hg[:, KEY_, :], hg[:, Q_, :]
                    else:
                        e.wait_ge(lev_sb.sem, lev_sb.after(l, n))
                        e.wait_ge(z_ok.sem, z_ok.after(l, n))
                        left = right = hg[:, Z0_ + n % 2, :]
                    for pair in range(HP):
                        for i in range(1 if n == 8 else TI):
                            c, o = pair * SEQ + i * P, (pair * TI + i) * P
                            if n not in (0, 8):
                                last = T.matmul(bank[4 + n % 2][:, o:o + P], left[:, c:c + P],
                                                apart[n % 2][:, pair * TI + i, :, :], start=True, stop=True)
                                continue
                            for hh in range(2):
                                if n == 8:
                                    c, o = pair * SEQ, pair * P
                                cr = c + P if n == 8 else c
                                last = T.matmul(bank[4 + hh][:, o:o + P], left[64 * hh:64 * hh + 64, c:c + P],
                                                right[64 * hh:64 * hh + 64, cr:cr + P], start=True, stop=True)
                    last.then_inc(lev_ps.sem, 1)

                def qk_transposes(i):
                    if i:
                        e.wait_ge(qkt_sb.sem, qkt_sb.after(l, 2))
                    e.wait_ge(qk_ok.sem, qk_ok.after(l, i + 1))
                    for j in range(2):
                        for hd in range(HA):
                            last = T.transpose(bank[6 + j][:, hd * P:hd * P + P], qk[:, j, i, hd * P:hd * P + P], ident[:, :])
                        last.then_inc(qkt_ps.sem, 1)

                def scores(i):
                    e.wait_ge(qkt_sb.sem, qkt_sb.after(l, 2 * i + 2))
                    n = (i + 1) * P
                    for hd in range(HA):
                        for c in range(2):
                            b, o = (2 + c, hd * n) if i == 0 else (2 * c + hd // 2, hd % 2 * n)
                            last = T.matmul(bank[b][:, o:o + n], qkT[64 * c:64 * c + 64, hd, i * P:i * P + P],
                                            qkT[64 * c:64 * c + 64, HA + hd, 0:n], start=True, stop=True)
                    last.then_inc(sc_ps.sem, 1)

                def project_out(i, tiles):
                    for k in tiles:
                        for half in range(2):
                            W = ring[:, WOUT[half], :].rearrange("p (k n) -> p k n", k=KT)
                            last = T.matmul(bank[2 * i + half][:, :], mixT[:, k, i * P:i * P + P], W[:, k, :],
                                            start=(k == 6), stop=(k == 3))
                            if k == 3:
                                last.then_inc(op_ps.sem, 1)

                e.wait_ge(ht_sb.sem, ht_sb.after(l, 4))
                W = section(0)
                project_columns(W, 4, 0)
                project_columns(W, 5, 1)
                W = section(1)
                project_rows(W, 6, 0)
                project_rows(W, 7, 1)
                proj_read(2)
                level(0)
                W = section(2)
                project_rows(W, 0, 0)
                level(1)
                project_rows(W, 1, 1)
                level(2)
                W = section(3)
                project_rows(W, 2, 0)
                level(3)
                proj_read(4)
                qk_transposes(0)
                project_rows(W, 3, 1)
                level(4)
                W = section(4)
                proj_read(5)
                project_rows(W, 0, 0)
                level(5)
                qk_transposes(1)
                proj_read(6)
                project_rows(W, 1, 1)
                level(6)
                proj_read(8)
                scores(0)
                W = section(5)
                proj_read(9)
                project_columns(W, 0, 0)
                level(7)
                proj_read(10)
                project_columns(W, 1, 1)
                level(8)
                proj_read(12)
                e.wait_ge(exp_ok.sem, exp_ok.after(l, 1))
                scores(1)
                e.wait_ge(qkt_sb.sem, qkt_sb.after(l, 4))
                e.wait_ge(w_ok.sem, w_ok.after(l, 1))
                for hd in range(HA):
                    last = T.transpose(bank[7][:, hd * P:hd * P + P], att_w[:, hd, 0:P], ident[:, :])
                last.then_inc(wt_ps.sem, 1)
                W = section(6)
                project_columns(W, 6, 0)
                e.wait_ge(lev_sb.sem, lev_sb.after(l, 9))
                e.wait_ge(wt_sb.sem, wt_sb.after(l, 1))
                for hd in range(HA):
                    last = T.matmul(bank[5][:, hd * DV:hd * DV + DV], wT[:, hd, :], av[:, 0, hd * DV:hd * DV + DV],
                                    start=True, stop=True)
                last.then_inc(pv_ps.sem, 1)
                for i in range(TI):
                    for hd in range(HB):
                        pair, hh, o = hd // 2, hd % 2, (i * HB + hd) * DB
                        last = T.matmul(bank[7][:, o:o + DB], sT[:, hh, pair * TI + i, :],
                                        bib[:, i, hd * DB:hd * DB + DB], start=True, stop=(i == 0))
                        if i:
                            last = T.matmul(bank[7][:, o:o + DB], far[:, hh, pair, :],
                                            bib[:, 0, hd * DB:hd * DB + DB], start=False, stop=True)
                last.then_inc(ob_ps.sem, 1)

                def oa_transposes(i):
                    e.wait_ge(oa_ok.sem, oa_ok.after(l, i + 1))
                    for hd in range(HA):
                        last = T.transpose(bank[5 + i][:, hd * P:hd * P + P], oa[:, i, hd * P:hd * P + P], ident[:, :])
                    last.then_inc(oat_ps.sem, 1)

                e.wait_ge(w_ok.sem, w_ok.after(l, 2))
                proj_read(13)
                for hd in (0, 1):
                    for c in range(TI):
                        last = T.transpose(bank[6][:, (2 * hd + c) * P:(2 * hd + c) * P + P],
                                           att_w[:, hd, c * P:c * P + P], ident[:, :])
                last.then_inc(wt_ps.sem, 1)
                for hd in (2, 3):
                    for c in range(TI):
                        o = (2 * (hd - 2) + c) * P
                        last = T.transpose(bank[4][:, o:o + P], att_w[:, hd, c * P:c * P + P], ident[:, :])
                last.then_inc(wt_ps.sem, 1)
                oa_transposes(0)
                e.wait_ge(ring_full[1].sem, ring_full[1].after(l, 32))
                e.wait_ge(ring_full[2].sem, ring_full[2].after(l, 32))
                e.wait_ge(exp_ok.sem, exp_ok.after(l, 2))
                e.wait_ge(conv_ok.sem, conv_ok.after(l, 1))
                project_out(0, (6, 7))
                e.wait_ge(ob_ok.sem, ob_ok.after(l, 1))
                e.wait_ge(wt_sb.sem, wt_sb.after(l, 3))
                for hd in range(HA):
                    for c in range(2):
                        last = T.matmul(bank[7][:, hd * DV:hd * DV + DV], wT[:, 4 + 2 * hd + c, :],
                                        av[:, c, hd * DV:hd * DV + DV], start=(c == 0), stop=(c == 1))
                last.then_inc(pv_ps.sem, 1)
                for i in range(TI):
                    for c in range(2):
                        last = T.transpose(bank[4][:, (c * TI + i) * P:(c * TI + i) * P + P],
                                           ob[:, i * 256 + c * P:i * 256 + c * P + P], ident[:, :])
                last.then_inc(obt_ps.sem, 1)
                e.wait_ge(oat_sb.sem, oat_sb.after(l, 1))
                e.wait_ge(obt_sb.sem, obt_sb.after(l, 1))
                project_out(0, (4, 5, 0, 1, 2, 3))
                project_out(1, (6, 7, 4, 5))
                oa_transposes(1)

                def router_logits(i):
                    if i == 0:
                        e.wait_ge(router_in.sem, router_in.after(l, 16 * 4))
                    for k in range(KT):
                        if k % 4 == 0:
                            e.wait_ge(ht_sb.sem, ht_sb.after(l, 5 + 2 * i + k // 4))
                        last = T.matmul(bank[4][:, i * 64:i * 64 + NE + NG], hT[:, k, i * P:i * P + P], wr[:, k, :],
                                        start=(k == 0), stop=(k == KT - 1))
                    if i == TI - 1:
                        last.then_inc(log_ps.sem, 1)

                def stream_rows(i):
                    e.wait_ge(x_mixed.sem, x_mixed.after(l, 2 * i + 2))
                    transposed_rows(i, x[:, i, :].rearrange("p (c k) -> p k c", k=KT))

                stream_rows(0)
                e.wait_ge(oat_sb.sem, oat_sb.after(l, 2))
                project_out(1, (0, 1, 2, 3))
                router_logits(0)
                stream_rows(1)
                router_logits(1)

                e.wait_ge(picks_ok.sem, picks_ok.after(l, 1))
                T.matmul(bank[5][:, 0:NE], before[:, :], picks[:, 0, :], start=True, stop=True)
                T.matmul(bank[5][:, NE:2 * NE], before[:, :], picks[:, 1, :], start=True, stop=False)
                T.matmul(bank[5][:, NE:2 * NE], ones[:, :], picks[:, 0, :], start=False, stop=True)
                T.matmul(bank[5][:, 2 * NE:3 * NE], ones[:, :], picks[:, 0, :], start=True, stop=False)
                T.matmul(bank[5][:, 2 * NE:3 * NE], ones[:, :], picks[:, 1, :], start=False, stop=True).then_inc(rank_ps.sem, 1)

                experts(main, l * GROUPS, OVERLAPPED, lambda i: FIRST[i], lambda s, i: ring_full[s].after(l, 16 * loads(s, i)))
                with e.Fori(1, GROUPS) as g:
                    experts(main, l * GROUPS + g, IN_TURN, slots_of,
                            lambda s, i: ring_full[s].after(l, 16 * (loads(s, UG - 1) + i // 2 - 1)) + g * 32)
                count, prior = extra_groups(e, l)
                with e.If(count > 0):
                    with e.Fori(0, count) as t:
                        e.wait_ge(main.x_added.sem, main.x_added.after(l * GROUPS + GROUPS, 0))
                        experts(extra, prior + t, IN_TURN, slots_of, lambda s, i: xring_full[s].after(prior + t, 16 * (i // 2 + 1)))
                layer_sums(e, l, count, prior)

        @block.scalar
        def _(e):
            A = nc.scalar.activation
            e.wait_ge(pro_dve.sem, 2)
            A(lbt, lbt, ACT.Exp).then_inc(pro_act.sem, 1)
            e.wait_ge(pro_dve.sem, 3)
            A(sinb[:, :, :], ang.rearrange("p (i n) -> p i n", i=TI), ACT.Sin)
            A(cosb[:, :, :], angc.rearrange("p (i n) -> p i n", i=TI), ACT.Sin).then_inc(pro_act.sem, 1)
            e.wait_ge(x_in.sem, 16)

            def experts(S, turn, order):
                e.wait_ge(S.gat_ps.sem, S.gat_ps.after(turn, 1))
                A(gatT, bank[2][:, 0:TI * P], ACT.Copy).then_inc(S.gat_sb.sem, 1)
                for part, i in order:
                    if part == "up":
                        e.wait_ge(S.gu_ps.sem, S.gu_ps.after(turn, i + 1))
                        A(sil[i % 2], bank[GU_BANK[i % 2]][:, 0:P], ACT.Exp, scale=-1.0).then_inc(S.gu_exp.sem, 1)
                        continue
                    e.wait_ge(S.at_ps.sem, S.at_ps.after(turn, i + 1))
                    A(actT, bank[3][:, 0:P], ACT.Copy).then_inc(S.at_sb.sem, 1)
                    e.wait_ge(S.ye_ps.sem, S.ye_ps.after(turn, i + 1))
                    for q in range(2):
                        last = A(ye[CAP * i:CAP * i + CAP, 2 * P * q:2 * P * q + 2 * P], bank[5][CAP * q:CAP * q + CAP, 0:2 * P], ACT.Copy)
                    last.then_inc(S.ye_act.sem, 1)

            with e.Fori(0, DEPTH) as l:

                def row_squares(n, i):
                    if n:
                        e.wait_ge(sums_ok.sem, sums_ok.after(l, n))
                    A(x_junk, x[:, i, :], ACT.Square, accum_out=ssq[:, i:i + 1]).then_inc(sums_ok.sem, 1)

                def copy_out(n):
                    b = (4, 5, 6, 7, 0, 1, 2, 3, 0, 1, 0, 1, 6)[n - 1]
                    e.wait_ge(proj_ps.sem, proj_ps.after(l, n))
                    A(u[:, n - 1, :], bank[b][:, :], ACT.Copy).then_inc(proj_sb.sem, 1)

                def decays(n):
                    if n >= 3:
                        e.wait_ge(lev_ps.sem, lev_ps.after(l, n - 1))
                    e.wait_ge(z_diff.sem, z_diff.after(l, n))
                    Z = hg[:, Z0_ + n % 2, :]
                    if n == 8:
                        zv, dv, gv = (t.rearrange("p (h c t) -> p h c t", c=4, t=CHUNK) for t in (Z, hg[:, D_, :], hg[:, G_, :]))
                        A(zv[:, :, 0:2, :], dv[:, :, 0:2, :], ACT.Exp, scale=-1.0)
                        A(zv[:, :, 2, :], gv[:, :, 2, :], ACT.Exp)
                        A(zv[:, :, 3, :], dv[:, :, 3, :], ACT.Exp).then_inc(z_exp.sem, 1)
                        return
                    zv, dv, gv = (t.rearrange("p (b o t) -> p b o t", o=2, t=LEVELS[n]) for t in (Z, hg[:, D_, :], hg[:, G_, :]))
                    A(zv[:, :, 0, :], dv[:, :, 0, :], ACT.Exp, scale=-1.0)
                    A(zv[:, :, 1, :], (gv if LEVELS[n] == CHUNK else dv)[:, :, 1, :], ACT.Exp).then_inc(z_exp.sem, 1)

                def qk_squares(i):
                    e.wait_ge(proj_sb.sem, proj_sb.after(l, 5 + i))
                    if i:
                        e.wait_ge(qk_ok.sem, qk_ok.after(l, 1))
                    A(smf[:, 0:2 * 512].rearrange("p (j n) -> p j n", j=2), qk[:, :, i, :], ACT.Square).then_inc(qk_sq.sem, 1)

                def qkt_out(i):
                    for j in range(2):
                        e.wait_ge(qkt_ps.sem, qkt_ps.after(l, 2 * i + j + 1))
                        A(qkT[:, HA * j:HA * j + HA, i * P:i * P + P], bank[6 + j][:, :].rearrange("p (h c) -> p h c", h=HA),
                          ACT.Copy).then_inc(qkt_sb.sem, 1)

                def softmax_exp(i):
                    if i:
                        e.wait_ge(w_ok.sem, w_ok.after(l, 1))
                    e.wait_ge(max_ok.sem, max_ok.after(l, i + 1))
                    n = (i + 1) * P
                    for m in range(HC):
                        b, o = (2 + m // HA, m % HA * n) if i == 0 else (2 * (m // HA) + m % HA // 2, m % 2 * n)
                        last = A(sm[:, m, 0:n], bank[b][:, o:o + n], ACT.Exp, bias=negmax[:, i * HC + m:i * HC + m + 1],
                                 scale=DK ** -0.5, accum_out=denom[:, i * HC + m:i * HC + m + 1])
                    last.then_inc(exp_ok.sem, 1)

                def wt_out(n):
                    e.wait_ge(wt_ps.sem, wt_ps.after(l, n + 1))
                    A(wT[:, 4 * n:4 * n + 4, :], bank[(7, 6, 4)[n]][:, :].rearrange("p (h c) -> p h c", h=4), ACT.Copy).then_inc(wt_sb.sem, 1)

                def oa_squares(i):
                    e.wait_ge(pv_ps.sem, pv_ps.after(l, i + 1))
                    if i:
                        e.wait_ge(oa_sq.sem, oa_sq.after(l, 1))
                    for hd in range(HA):
                        last = A(oa_junk[:, hd, :], bank[(5, 7)[i]][:, hd * DV:hd * DV + DV], ACT.Square,
                                 accum_out=oa_ms[:, 4 * i + hd:4 * i + hd + 1])
                    last.then_inc(oa_sq.sem, 1)

                A(warm, eps, ACT.Exp)
                e.wait_ge(stream_ok.sem, stream_ok.after(l, 1))
                for i in range(TI):
                    row_squares(i, i)
                copy_out(1)
                e.wait_ge(proj_sb.sem, proj_sb.after(l, 1))
                A(hg[:, Z0_, :], bq, ACT.Exp, scale=-1.0).then_inc(hg_act.sem, 1)
                copy_out(2)
                e.wait_ge(hg_dve.sem, hg_dve.after(l, 1))
                A(hg[:, Z0_ + 1, :], hg[:, D_, :], ACT.Exp, scale=-1.0).then_inc(hg_act.sem, 1)
                e.wait_ge(hg_dve.sem, hg_dve.after(l, 2))
                A(hg[:, G_, :], hg[:, G_, :], ACT.Ln)
                A(hg[:, Z0_, :], hg[:, Z0_, :], ACT.Ln, scale=1.0 / LN_CUT).then_inc(hg_act.sem, 1)
                e.wait_ge(lam_sum.sem, lam_sum.after(l, 1))
                A(lam_e, lam_s, ACT.Exp).then_inc(lam_exp.sem, 1)
                copy_out(3)
                copy_out(4)
                decays(1)
                decays(2)
                copy_out(5)
                qk_squares(0)
                decays(3)
                copy_out(6)
                decays(4)
                qk_squares(1)
                copy_out(7)
                decays(5)
                qkt_out(0)
                copy_out(8)
                decays(6)
                copy_out(9)
                decays(7)
                qkt_out(1)
                copy_out(10)
                decays(8)
                e.wait_ge(proj_sb.sem, proj_sb.after(l, 10))
                e.wait_ge(z_exp.sem, z_exp.after(l, 8))
                A(egate.rearrange("p (i n) -> p i n", i=TI), bib[:, :, HB * DB:2 * HB * DB], ACT.Exp, scale=-1.0).then_inc(gate_exp.sem, 1)
                softmax_exp(0)
                copy_out(11)
                copy_out(12)
                wt_out(0)
                softmax_exp(1)
                copy_out(13)
                oa_squares(0)
                e.wait_ge(conv_in.sem, conv_in.after(l, 1))
                for back, tap in ((0, cxT), (1, bq), (2, bf)):
                    for ct in range(2):
                        w = 4 + 2 * (2 - back) + ct
                        last = A(tap[:, ct * SEQ:ct * SEQ + SEQ], ccT[:, ct * SEQ:ct * SEQ + SEQ], ACT.Copy, scale=cur[:, w:w + 1])
                last.then_inc(taps_ok.sem, 1)
                e.wait_ge(ob_ps.sem, ob_ps.after(l, 1))
                for m in range(TI * HB):
                    last = A(ob_junk[:, m, :], bank[7][:, m * DB:m * DB + DB], ACT.Square, accum_out=ob_ms[:, m:m + 1])
                last.then_inc(ob_sq.sem, 1)
                wt_out(1)
                wt_out(2)

                def oat_out(i):
                    e.wait_ge(oat_ps.sem, oat_ps.after(l, i + 1))
                    A(mixT[:, 0:4, i * P:i * P + P], bank[5 + i][:, :].rearrange("p (h c) -> p h c", h=4), ACT.Copy).then_inc(oat_sb.sem, 1)

                oat_out(0)
                oa_squares(1)
                e.wait_ge(obt_ps.sem, obt_ps.after(l, 1))
                A(mixT[:, 4:6, :], bank[4][:, :].rearrange("p (c t) -> p c t", c=2), ACT.Copy).then_inc(obt_sb.sem, 1)
                oat_out(1)
                for i in range(TI):
                    e.wait_ge(x_mixed.sem, x_mixed.after(l, 2 * i + 2))
                    row_squares(TI + i, i)
                e.wait_ge(top_g.sem, top_g.after(l, 1))
                for i in range(TI):
                    last = A(rjunk[:, i, :], lg[:, i, NE:NE + NG], ACT.Exp, bias=nmg[:, i:i + 1], accum_out=expsum[:, i:i + 1])
                last.then_inc(exp_g.sem, 1)
                e.wait_ge(top_e.sem, top_e.after(l, 1))
                A(edif, edif, ACT.Exp).then_inc(exp_e.sem, 1)

                experts(main, l * GROUPS, OVERLAPPED)
                e.wait_ge(routed.sem, routed.after(l, 1))
                settle(e)
                with e.If(l < DEPTH - 1):
                    after = nc.s_assert_within(l + 1, 1, DEPTH - 1)
                    mixer_parameters(e, after)
                    router_parameters(e, after)
                count, prior = extra_groups(e, l)
                with e.Fori(1, GROUPS) as g:
                    experts(main, l * GROUPS + g, IN_TURN)
                with e.If(count > 0):
                    with e.Fori(0, count) as t:
                        e.wait_ge(main.x_added.sem, main.x_added.after(l * GROUPS + GROUPS, 0))
                        experts(extra, prior + t, IN_TURN)

        @block.vector
        def _(e):
            V = nc.vector
            TT, TS, STT = V.tensor_tensor, V.tensor_scalar, V.scalar_tensor_tensor
            for S in (main, extra):
                e.sem_inc(S.x_added.sem, 1)
                e.sem_inc(S.dve.sem, 1)
            c = Chain(pro_dve, 0)
            e.wait_ge(pro_pe.sem, 1)
            V.tensor_copy(pcol[:, :], bank[0][:, 0:DEPTH * 8]).then_inc(c.step(), 1)
            e.wait_ge(c.sem, c.last())
            lb_raw = pcol[:, 0:DEPTH * HP].rearrange("p (l h) -> p h l", l=DEPTH)
            lbl = lbt.rearrange("p (l h) -> p l h", l=DEPTH)
            e.wait_ge(const_ok.sem, IDENT_MADE)
            prol = Chain(dve_p, 0)
            V.tensor_reduce(lbm, lb_raw, AX, ALU.max).then_inc(prol.step(), 1)
            e.wait_ge(prol.sem, prol.last())
            TT(lbl, pcol[:, 0:DEPTH * HP].rearrange("p (l h) -> p l h", l=DEPTH), lbm.unsqueeze(1).to_broadcast([P, DEPTH, HP]), ALU.subtract).then_inc(c.step(), 1)
            e.wait_ge(pos_in.sem, 16)
            angv = ang.rearrange("p (i n) -> p i n", i=TI)
            V.tensor_copy(pos_f, pos_i[:, :]).then_inc(prol.step(), 1)
            e.wait_ge(prol.sem, prol.last())
            TT(angv, pos_f.unsqueeze(2).to_broadcast([P, TI, HALF]), freq.unsqueeze(1).to_broadcast([P, TI, HALF]), ALU.mult).then_inc(prol.step(), 1)
            e.wait_ge(prol.sem, prol.last())
            parts, rest = [], 2 * math.pi
            for unit_ in (0.25, 2.0 ** -5, 2.0 ** -13, 2.0 ** -17):
                parts.append(math.floor(rest / unit_) * unit_)
                rest -= parts[-1]
            parts.append(rest)
            for _ in range(2):
                TS(turn_n, ang, 1.0 / (2 * math.pi), 12582912.0, ALU.mult, ALU.add).then_inc(prol.step(), 1)
                e.wait_ge(prol.sem, prol.last())
                TS(turn_n, turn_n, -12582912.0, None, ALU.add).then_inc(prol.step(), 1)
                e.wait_ge(prol.sem, prol.last())
                for part in parts:
                    STT(ang, turn_n, -part, ang, ALU.mult, ALU.add).then_inc(prol.step(), 1)
                    e.wait_ge(prol.sem, prol.last())
            PI = 3.1415925
            TS(angc, ang, math.pi / 2, None, ALU.add).then_inc(prol.step(), 1)
            TS(ang, ang, PI, -PI, ALU.min, ALU.max).then_inc(prol.step(), 1)
            e.wait_ge(prol.sem, prol.last())
            TS(turn_n, angc, math.pi, -2 * math.pi, ALU.is_gt, ALU.mult).then_inc(prol.step(), 1)
            e.wait_ge(prol.sem, prol.last())
            TT(angc, angc, turn_n, ALU.add).then_inc(prol.step(), 1)
            e.wait_ge(prol.sem, prol.last())
            TS(angc, angc, PI, -PI, ALU.min, ALU.max).then_inc(c.step(), 1)
            e.wait_ge(pro_act.sem, 1)
            V.tensor_reduce(lbs, lbt.rearrange("p (l h) -> p h l", l=DEPTH), AX, ALU.add).then_inc(prol.step(), 1)
            V.memset(table[:, 0, 0:HP], 0.0).then_inc(prol.step(), 1)
            e.wait_ge(prol.sem, prol.last())
            V.reciprocal(lbs, lbs).then_inc(prol.step(), 1)
            e.wait_ge(prol.sem, prol.last())
            TT(lbl, lbl, lbs.unsqueeze(1).to_broadcast([P, DEPTH, HP]), ALU.mult).then_inc(prol.step(), 1)
            e.wait_ge(prol.sem, prol.last())
            for n in range(1, DEPTH):
                TT(table[:, n, 0:HP], table[:, n - 1, 0:HP], lbl[:, n, :], ALU.add).then_inc(prol.step(), 1)
                e.wait_ge(prol.sem, prol.last())
            TS(table[:, :, HP:2 * HP], table[:, :, 0:HP], -1.0, 1.0, ALU.mult, ALU.add).then_inc(prol.step(), 1)
            V.tensor_copy(table[:, :, 4:10], pcol[:, DEPTH * HP:DEPTH * 8].rearrange("p (l j) -> p l j", l=DEPTH)).then_inc(prol.step(), 1)
            e.wait_ge(prol.sem, prol.last())
            e.wait_ge(const_ok.sem, CONSTS)
            e.wait_ge(pro_act.sem, 2)

            def experts(S, turn, order, codes, meanwhile=None):
                c = Chain(S.dve, turn)
                e.wait_ge(c.sem, c.last())
                for i in range(TI):
                    TS(sel[:, i, :], iota[:, :], codes[:, i:i + 1], None, ALU.is_equal).then_inc(c.step(), 1)
                for i in range(TI):
                    TS(gat[:, i, :], iota[:, :], codes[:, i:i + 1], gates[:, i:i + 1], ALU.is_equal, ALU.mult).then_inc(c.step(), 1)
                e.wait_ge(c.sem, c.last() - TI)
                for i in range(TI):
                    last = STT(sel[:, i, :], iota[:, :], codes[:, TI + i:TI + i + 1], sel[:, i, :], ALU.is_equal, ALU.add)
                    if i < TI - 1:
                        last.then_inc(c.step(), 1)
                last.then_inc(S.sel_ok.sem, 1)
                for i in range(TI):
                    TS(gtmp[:, i, :], iota[:, :], codes[:, TI + i:TI + i + 1], gates[:, TI + i:TI + i + 1], ALU.is_equal, ALU.mult).then_inc(c.step(), 1)
                e.wait_ge(c.sem, c.last())
                TT(gat, gat, gtmp, ALU.add).then_inc(S.gat_ok.sem, 1)
                TS(codes, codes, -float(UG * CAP), None, ALU.add).then_inc(c.step(), 1)
                if meanwhile:
                    meanwhile()
                for half in range(2):
                    e.wait_ge(S.gath_ps.sem, S.gath_ps.after(turn, half + 1))
                    TT(xg[:, 4 * half:4 * half + 4, :], bank[half][:, :].rearrange("p (k c) -> p k c", k=4),
                       gffn[:, 4 * half:4 * half + 4].unsqueeze(2).to_broadcast([P, 4, P]), ALU.mult).then_inc(S.xg_ok.sem, 1)
                for part, i in order:
                    if part == "up":
                        gu, r = bank[GU_BANK[i % 2]], silr[i % 2]
                        e.wait_ge(S.gu_exp.sem, S.gu_exp.after(turn, i + 1))
                        TS(r, sil[i % 2], 1.0, None, ALU.add).then_inc(c.step(), 1)
                        e.wait_ge(c.sem, c.last())
                        V.reciprocal(r, r).then_inc(c.step(), 1)
                        e.wait_ge(c.sem, c.last())
                        TT(r, gu[:, 0:P], r, ALU.mult).then_inc(c.step(), 1)
                        e.wait_ge(c.sem, c.last())
                        TT(actv[i % 2], gu[:, P:2 * P], r, ALU.mult).then_inc(S.act_ok.sem, 1)
                        continue
                    e.wait_ge(S.ye_ps.sem, S.ye_ps.after(turn, i + 1))
                    for q in range(2, 4):
                        last = V.tensor_copy(ye[CAP * i:CAP * i + CAP, 2 * P * q:2 * P * q + 2 * P], bank[5][CAP * q:CAP * q + CAP, 0:2 * P])
                    last.then_inc(S.ye_dve.sem, 1)
                for n in range(4):
                    e.wait_ge(S.scat_ps.sem, S.scat_ps.after(turn, n + 1))
                    xs = x[:, n // 2, n % 2 * 512:n % 2 * 512 + 512]
                    TT(xs, bank[(6, 7, 0, 1)[n]][:, :], xs, ALU.add).then_inc(S.x_added.sem, 1)
                c.end()

            e.wait_ge(x_in.sem, 16)
            with e.Fori(0, DEPTH) as l:
                c = Chain(dve_m, l)

                def rsqrt(dst, sums, n, between=()):
                    other = list(between)
                    m = sums.shape[1]
                    v, vh, w = rs_v[:, 0:m], rs_h[:, 0:m], rs_w[:, 0:m]
                    TS(v, sums, 1.0 / n, EPS, ALU.mult, ALU.add).then_inc(c.step(), 1)
                    TS(vh, sums, -0.5 / n, -0.5 * EPS, ALU.mult, ALU.add).then_inc(c.step(), 1)
                    if other:
                        other.pop(0)()
                    e.wait_ge(c.sem, c.last())
                    TS(dst.bitcast(I32), v.bitcast(I32), -0.5, float(0x5F3759DF), ALU.mult, ALU.add).then_inc(c.step(), 1)
                    for _ in range(3):
                        if other:
                            other.pop(0)()
                        e.wait_ge(c.sem, c.last())
                        TT(w, dst, dst, ALU.mult).then_inc(c.step(), 1)
                        e.wait_ge(c.sem, c.last())
                        TT(w, w, vh, ALU.mult).then_inc(c.step(), 1)
                        e.wait_ge(c.sem, c.last())
                        STT(dst, w, 1.5, dst, ALU.add, ALU.mult).then_inc(c.step(), 1)
                    e.wait_ge(c.sem, c.last())

                def normed(i):
                    return TS(h[:, i, :, :], x[:, i, :].rearrange("p (c k) -> p k c", k=KT), rstd[:, i:i + 1], None, ALU.mult)

                def take_transposed(n, gain):
                    i, half = n % 4 // 2, n % 2
                    e.wait_ge(ht_ps.sem, ht_ps.after(l, n + 1))
                    TT(hT[:, 4 * half:4 * half + 4, i * P:i * P + P], bank[n % 4][:, :].rearrange("p (k c) -> p k c", k=4),
                       gain[:, 4 * half:4 * half + 4].unsqueeze(2).to_broadcast([P, 4, P]), ALU.mult).then_inc(ht_sb.sem, 1)

                def mixer_norm():
                    e.wait_ge(sums_ok.sem, sums_ok.after(l, 2))
                    rsqrt(rstd, ssq, D)
                    for i in range(TI):
                        normed(i).then_inc(h_ok.sem, 1)
                    for n in range(4):
                        take_transposed(n, gmix)
                    V.memset(sT, 0.0).then_inc(c.step(), 1)

                def residual(i):
                    for half in range(2):
                        e.wait_ge(op_ps.sem, op_ps.after(l, 2 * i + half + 1))
                        xs = x[:, i, half * 512:half * 512 + 512]
                        TT(xs, bank[2 * i + half][:, :], xs, ALU.add).then_inc(x_mixed.sem, 1)

                def start_of_layer():
                    V.tensor_copy(cur[:, :].unsqueeze(1), table[:, ds(l, 1), :]).then_inc(c.step(), 1)
                    V.tensor_copy(gffn[:, :], gffn_in[:, :]).then_inc(c.step(), 1)
                    lv = lamv[:, :, :].rearrange("p (a b) n -> p a b n", b=2)
                    prod = hg[:, G_, 0:2 * DK].rearrange("p (a n) -> p a n", a=2)
                    TT(prod, lv[:, :, 0, :], lv[:, :, 1, :], ALU.mult).then_inc(c.step(), 1)
                    e.wait_ge(c.sem, c.last())
                    V.tensor_reduce(lam_s, prod, AX, ALU.add).then_inc(lam_sum.sem, 1)
                    TS(subs, cur[:, 10:11], -1.0, 1.0, ALU.mult, ALU.add).then_inc(c.step(), 1)
                    e.wait_ge(c.sem, c.last())
                    TS(subgl[:, :], subg[:, :], subs, None, ALU.mult).then_inc(c.step(), 1)

                def hgrn_inputs():
                    G, Q, K, Dt, A0, A1 = (hg[:, n, :] for n in range(6))
                    e.wait_ge(hg_act.sem, hg_act.after(l, 1))
                    TS(A0, A0, 1.0, None, ALU.add).then_inc(c.step(), 1)
                    e.wait_ge(c.sem, c.last())
                    V.reciprocal(A0, A0).then_inc(c.step(), 1)
                    e.wait_ge(proj_sb.sem, proj_sb.after(l, 2))
                    TS(Dt, bf, -80.0, None, ALU.max).then_inc(hg_dve.sem, 1)
                    e.wait_ge(c.sem, c.last())
                    TT(Q, bq, A0, ALU.mult).then_inc(c.step(), 1)
                    e.wait_ge(hg_act.sem, hg_act.after(l, 2))
                    e.wait_ge(c.sem, c.last())
                    TS(A0, A1, 1.0, None, ALU.add).then_inc(c.step(), 1)
                    e.wait_ge(c.sem, c.last())
                    V.reciprocal(A0, A0).then_inc(c.step(), 1)
                    e.wait_ge(c.sem, c.last())
                    TT(A1, A1, A0, ALU.mult).then_inc(c.step(), 1)
                    for p in range(HP):
                        s = slice(p * SEQ, p * SEQ + SEQ)
                        TS(Dt[:, s], A0[:, s], cur[:, HP + p:HP + p + 1], cur[:, p:p + 1], ALU.mult, ALU.add).then_inc(c.step(), 1)
                    e.wait_ge(c.sem, c.last())
                    TS(G, Dt, LN_CUT, None, ALU.max).then_inc(c.step(), 1)
                    TS(A0, Dt, TINY, LN_CUT, ALU.max, ALU.min).then_inc(hg_dve.sem, 1)
                    for p in range(HP):
                        s = slice(p * SEQ, p * SEQ + SEQ)
                        last = TS(K[:, s], A1[:, s], cur[:, HP + p:HP + p + 1], None, ALU.mult)
                        if p < HP - 1:
                            last.then_inc(c.step(), 1)
                    last.then_inc(hg_qk.sem, 1)
                    e.wait_ge(hg_act.sem, hg_act.after(l, 3))
                    TT(Dt, G, A0, ALU.add).then_inc(c.step(), 1)
                    e.wait_ge(c.sem, c.last())
                    V.tensor_tensor_scan(out=G, data0=restart[:, :, :].rearrange("p h t -> p (h t)"), data1=Dt,
                                         initial=0.0, op0=ALU.mult, op1=ALU.add).then_inc(c.step(), 1)
                    e.wait_ge(c.sem, c.last())

                def differences(n):
                    if n > 1:
                        e.wait_ge(z_exp.sem, z_exp.after(l, n - 1))
                    if n == 8:
                        gv, dv = (t.rearrange("p (h c t) -> p h c t", c=4, t=CHUNK) for t in (hg[:, G_, :], hg[:, D_, :]))
                        TT(dv[:, :, 0:2, :], gv[:, :, 0:2, :], gv[:, :, 0:2, CHUNK - 1:CHUNK].to_broadcast([P, HP, 2, CHUNK]), ALU.subtract).then_inc(c.step(), 1)
                        e.wait_ge(c.sem, c.last())
                        TT(dv[:, :, 0, :], dv[:, :, 0, :], gv[:, :, 1, CHUNK - 1:CHUNK].to_broadcast([P, HP, CHUNK]), ALU.subtract).then_inc(c.step(), 1)
                        TT(dv[:, :, 3, :], gv[:, :, 3, :], gv[:, :, 2, CHUNK - 1:CHUNK].to_broadcast([P, HP, CHUNK]), ALU.add).then_inc(z_diff.sem, 1)
                        return
                    B = LEVELS[n]
                    nb = HP * SEQ // (2 * B)
                    gv, dv = (t.rearrange("p (b t) -> p b t", t=2 * B) for t in (hg[:, G_, :], hg[:, D_, :]))
                    w = B if B == CHUNK else 2 * B
                    TT(dv[:, :, 0:w], gv[:, :, 0:w], gv[:, :, B - 1:B].to_broadcast([P, nb, w]), ALU.subtract).then_inc(z_diff.sem, 1)

                def scaled(n):
                    e.wait_ge(z_exp.sem, z_exp.after(l, n))
                    Z = hg[:, Z0_ + n % 2, :]
                    w = P if n == 8 else LEVELS[n]
                    zv, kv, qv = (t.rearrange("p (b o t) -> p b o t", o=2, t=w) for t in (Z, hg[:, KEY_, :], hg[:, Q_, :]))
                    TT(zv[:, :, 0, :], zv[:, :, 0, :], kv[:, :, 0, :], ALU.mult).then_inc(c.step(), 1)
                    if n == 8:
                        TT(zv[:, :, 1, :], zv[:, :, 1, :], qv[:, :, 1, :], ALU.mult).then_inc(z_ok.sem, 1)
                        return
                    for hh in range(2):
                        rows = slice(64 * hh, 64 * hh + 64)
                        z2, q2 = (t[rows, :].rearrange("p (m b o t) -> p m b o t", m=HP * TI, o=2, t=w)[:, :, :, 1, :]
                                  for t in (Z, hg[:, Q_, :]))
                        last = TT(apart[n % 2][rows, :, hh, :].rearrange("p m (b t) -> p m b t", t=w), z2, q2, ALU.mult)
                        if hh == 0:
                            last.then_inc(c.step(), 1)
                    last.then_inc(z_ok.sem, 1)

                def take_level(n):
                    e.wait_ge(lev_ps.sem, lev_ps.after(l, n + 1))
                    settle(e)
                    for hh in range(2):
                        if n == 8:
                            last = V.tensor_copy(far[:, hh, :, :], bank[4 + hh][:, 0:HP * P].rearrange("p (h t) -> p h t", h=HP))
                        elif n == 0:
                            last = V.copy_predicated(sT[:, hh, :, :], masks[:, n:n + 1, :].bitcast(I32).to_broadcast([P, HP * TI, P]),
                                                     bank[4 + hh][:, :].rearrange("p (h t) -> p h t", t=P))
                        else:
                            B = LEVELS[n]
                            nb = P // (2 * B)
                            second = lambda v: v.rearrange("p h (b o t) -> p h b o t", o=2, t=B)[:, :, :, 1, :]
                            last = V.copy_predicated(
                                second(sT[:, hh, :, :]),
                                second(masks[:, n:n + 1, :].bitcast(I32)).to_broadcast([P, HP * TI, nb, B]),
                                bank[4 + n % 2][:, :].rearrange("p (h a b t) -> p h a b t", a=2, b=nb, t=B)[:, :, hh, :, :])
                        if hh == 0:
                            last.then_inc(c.step(), 1)
                    last.then_inc(lev_sb.sem, 1)

                def qk_finish(i):
                    e.wait_ge(qk_sq.sem, qk_sq.after(l, i + 1))
                    V.tensor_reduce(qk_ms, smf[:, 0:2 * 512].rearrange("p (m d) -> p m d", d=DK), AX, ALU.add).then_inc(c.step(), 1)
                    e.wait_ge(c.sem, c.last())
                    rsqrt(qk_rs, qk_ms, DK)
                    v = qk[:, :, i, :].rearrange("p j (m d) -> p j m d", d=DK)
                    TT(v, v, qk_rs.rearrange("p (j m) -> p j m", j=2).unsqueeze(3).to_broadcast([P, 2, HC, DK]), ALU.mult).then_inc(c.step(), 1)
                    e.wait_ge(c.sem, c.last())
                    TT(v, v, qkg[:, :, :].unsqueeze(2).to_broadcast([P, 2, HC, DK]), ALU.mult).then_inc(c.step(), 1)
                    e.wait_ge(c.sem, c.last())
                    t1, t2 = v[:, :, :, 0:HALF], v[:, :, :, HALF:2 * HALF]
                    w = 2 * HC * HALF
                    t1c, t2s, t1s, t2c = (smf[:, n * w:n * w + w].rearrange("p (j m d) -> p j m d", j=2, d=HALF) for n in range(4))
                    cv, sv = (t[:, i:i + 1, :].unsqueeze(1).to_broadcast([P, 2, HC, HALF]) for t in (cosb, sinb))
                    TT(t1c, t1, cv, ALU.mult).then_inc(c.step(), 1)
                    TT(t2s, t2, sv, ALU.mult).then_inc(c.step(), 1)
                    TT(t1s, t1, sv, ALU.mult).then_inc(c.step(), 1)
                    TT(t2c, t2, cv, ALU.mult).then_inc(c.step(), 1)
                    e.wait_ge(c.sem, c.last())
                    TT(t1, t1c, t2s, ALU.subtract).then_inc(c.step(), 1)
                    TT(t2, t1s, t2c, ALU.add).then_inc(qk_ok.sem, 1)

                def softmax_max(i):
                    e.wait_ge(sc_ps.sem, sc_ps.after(l, i + 1))
                    n = (i + 1) * P
                    banks = (2, 3) if i == 0 else (0, 1, 2, 3)
                    maps = HC // len(banks)
                    for b in banks:
                        v = bank[b][:, :].rearrange("p (m n) -> p m n", m=maps)[:, :, n - CHUNK:n]
                        TT(v, v, attn_mask[:, :].unsqueeze(1).to_broadcast([P, maps, CHUNK]), ALU.add).then_inc(c.step(), 1)
                    e.wait_ge(c.sem, c.last())
                    nm = negmax[:, i * HC:i * HC + HC]
                    for m, b in enumerate(banks):
                        V.tensor_reduce(nm[:, m * maps:m * maps + maps], bank[b][:, :].rearrange("p (m n) -> p m n", m=maps), AX, ALU.max).then_inc(c.step(), 1)
                    e.wait_ge(c.sem, c.last())
                    TS(nm, nm, -DK ** -0.5, None, ALU.mult).then_inc(max_ok.sem, 1)

                def attention_weights(i):
                    e.wait_ge(exp_ok.sem, exp_ok.after(l, i + 1))
                    n, r = (i + 1) * P, inv[:, i * HC:i * HC + HC]
                    V.reciprocal(r, denom[:, i * HC:i * HC + HC]).then_inc(c.step(), 1)
                    e.wait_ge(c.sem, c.last())
                    TS(r[:, HA:HC], r[:, HA:HC], nlam, None, ALU.mult).then_inc(c.step(), 1)
                    e.wait_ge(c.sem, c.last())
                    TT(sm[:, :, 0:n], sm[:, :, 0:n], r.unsqueeze(2).to_broadcast([P, HC, n]), ALU.mult).then_inc(c.step(), 1)
                    if i:
                        e.wait_ge(wt_ps.sem, wt_ps.after(l, 1))
                    e.wait_ge(c.sem, c.last())
                    TT(att_w[:, :, 0:n], sm[:, 0:HA, 0:n], sm[:, HA:HC, 0:n], ALU.add).then_inc(w_ok.sem, 1)

                def oa_finish(i):
                    e.wait_ge(oa_sq.sem, oa_sq.after(l, i + 1))
                    rs = oa_rs[:, 4 * i:4 * i + 4]
                    rsqrt(rs, oa_ms[:, 4 * i:4 * i + 4], DV)
                    v = oa[:, i, :].rearrange("p (h d) -> p h d", d=DV)
                    TT(v, bank[(5, 7)[i]][:, :].rearrange("p (h d) -> p h d", d=DV),
                       rs.unsqueeze(2).to_broadcast([P, HA, DV]), ALU.mult).then_inc(c.step(), 1)
                    e.wait_ge(c.sem, c.last())
                    TT(v, v, subgl[:, :].unsqueeze(1).to_broadcast([P, HA, DV]), ALU.mult).then_inc(oa_ok.sem, 1)

                e.sem_inc(stream_ok.sem, 1)
                e.wait_ge(params_in.sem, params_in.after(l, 16 * 10))
                start_of_layer()
                mixer_norm()
                hgrn_inputs()
                V.memset(u[:, 0:2, :], 0.0).then_inc(c.step(), 1)
                e.wait_ge(c.sem, c.last())
                differences(1)
                differences(2)
                scaled(1)
                scaled(2)
                take_level(0)
                differences(3)
                take_level(1)
                differences(4)
                qk_finish(0)
                scaled(3)
                take_level(2)
                differences(5)
                scaled(4)
                qk_finish(1)
                take_level(3)
                differences(6)
                scaled(5)
                take_level(4)
                differences(7)
                scaled(6)
                take_level(5)
                differences(8)
                scaled(7)
                take_level(6)
                scaled(8)
                e.wait_ge(lam_exp.sem, lam_exp.after(l, 1))
                TT(nlam, lam_e[:, 1:2], lam_e[:, 0:1], ALU.subtract).then_inc(c.step(), 1)
                e.wait_ge(c.sem, c.last())
                TT(nlam, nlam, cur[:, 10:11], ALU.subtract).then_inc(c.step(), 1)
                softmax_max(0)
                take_level(7)
                attention_weights(0)
                take_level(8)
                softmax_max(1)
                e.wait_ge(gate_sum.sem, gate_sum.after(l, 1))
                V.reciprocal(egate, egate).then_inc(gate_rec.sem, 1)
                attention_weights(1)
                oa_finish(0)
                e.wait_ge(ob_sq.sem, ob_sq.after(l, 1))
                rsqrt(ob_rs, ob_ms, DB)
                obv = ob.rearrange("p (m d) -> p m d", d=DB)
                TT(obv, bank[7][:, :].rearrange("p (m d) -> p m d", d=DB), ob_rs.unsqueeze(2).to_broadcast([P, TI * HB, DB]),
                   ALU.mult).then_inc(c.step(), 1)
                e.wait_ge(c.sem, c.last())
                TT(obv, obv, hng[:, :].unsqueeze(1).to_broadcast([P, TI * HB, DB]), ALU.mult).then_inc(c.step(), 1)
                e.wait_ge(c.sem, c.last())
                e.wait_ge(gate_ok.sem, gate_ok.after(l, 1))
                TT(ob, ob, egate, ALU.mult).then_inc(ob_ok.sem, 1)
                oa_finish(1)
                for i in range(TI):
                    residual(i)
                    e.wait_ge(sums_ok.sem, sums_ok.after(l, 2 + i + 1))
                    rsqrt(rstd[:, i:i + 1], ssq[:, i:i + 1], D,
                          [lambda n=4 + 2 * i + half: take_transposed(n, gffn) for half in range(2)])
                normed(0).then_inc(h_ok.sem, 1)
                e.wait_ge(router_in.sem, router_in.after(l, 16 * 4))
                e.wait_ge(log_ps.sem, log_ps.after(l, 1))
                logits = bank[4][:, 0:TI * 64].rearrange("p (i n) -> p i n", i=TI)
                V.memset(lg[:, :, NE + NG:NE + 8], -3.0e38).then_inc(c.step(), 1)
                for i in range(TI):
                    STT(lg[:, i, 0:NE + NG], logits[:, i, 0:NE + NG], rstd[:, i:i + 1], rb[:, :], ALU.mult, ALU.add).then_inc(c.step(), 1)
                e.wait_ge(c.sem, c.last())
                settle(e)
                for i in range(TI):
                    V.max(mg[:, i, :], lg[:, i, NE:NE + 8]).then_inc(c.step(), 1)
                e.wait_ge(c.sem, c.last())
                settle(e)
                for i in range(TI):
                    V.max_index(idx[:, i, :], mg[:, i, :], lg[:, i, NE:NE + 8]).then_inc(c.step(), 1)
                TS(nmg, mg[:, :, 0], -1.0, None, ALU.mult).then_inc(top_g.sem, 1)
                e.wait_ge(c.sem, c.last())
                V.tensor_copy(gidx, idx[:, 0:TI, 0]).then_inc(c.step(), 1)
                e.wait_ge(c.sem, c.last())
                TT(ohg, iota[:, 0:NG].unsqueeze(1).to_broadcast([P, TI, NG]), gidx.unsqueeze(2).to_broadcast([P, TI, NG]), ALU.is_equal).then_inc(c.step(), 1)
                e.wait_ge(c.sem, c.last())
                TS(pen, ohg, 1.0e30, -1.0e30, ALU.mult, ALU.add).then_inc(c.step(), 1)
                lge = lg[:, :, 0:NE].rearrange("p i (g n) -> p i g n", g=NG)
                emv = em.rearrange("p i (g n) -> p i g n", g=NG)
                e.wait_ge(c.sem, c.last())
                TT(emv, lge, pen.unsqueeze(3).to_broadcast([P, TI, NG, EPG]), ALU.add).then_inc(c.step(), 1)
                e.wait_ge(c.sem, c.last())
                settle(e)
                for i in range(TI):
                    V.max(mv[:, i, :], em[:, i, :]).then_inc(c.step(), 1)
                e.wait_ge(c.sem, c.last())
                settle(e)
                for i in range(TI):
                    V.max_index(idx[:, TI + i, :], mv[:, i, :], em[:, i, :]).then_inc(c.step(), 1)
                TT(edif, mv[:, :, 1], mv[:, :, 0], ALU.subtract).then_inc(top_e.sem, 1)
                e.wait_ge(c.sem, c.last())
                V.tensor_copy(eid, idx[:, TI:2 * TI, 0:NK].rearrange("p i k -> p k i")).then_inc(c.step(), 1)
                e.wait_ge(c.sem, c.last())
                TT(oh, iota[:, 0:NE].unsqueeze(1).to_broadcast([P, NK * TI, NE]),
                   eidf.unsqueeze(2).to_broadcast([P, NK * TI, NE]), ALU.is_equal).then_inc(c.step(), 1)
                e.wait_ge(c.sem, c.last())
                TT(picks, oh[:, 0:TI, :], oh[:, TI:2 * TI, :], ALU.add).then_inc(picks_ok.sem, 1)
                normed(1).then_inc(h_ok.sem, 1)
                e.wait_ge(exp_g.sem, exp_g.after(l, 1))
                e.wait_ge(exp_e.sem, exp_e.after(l, 1))
                TS(gates[:, TI:2 * TI], edif, 1.0, None, ALU.add).then_inc(c.step(), 1)
                e.wait_ge(c.sem, c.last())
                TT(gates[:, TI:2 * TI], gates[:, TI:2 * TI], expsum, ALU.mult).then_inc(c.step(), 1)
                e.wait_ge(c.sem, c.last())
                V.reciprocal(gates[:, 0:TI], gates[:, TI:2 * TI]).then_inc(c.step(), 1)
                e.wait_ge(c.sem, c.last())
                TT(gates[:, TI:2 * TI], gates[:, 0:TI], edif, ALU.mult).then_inc(c.step(), 1)
                e.wait_ge(rank_ps.sem, rank_ps.after(l, 1))
                rk = bank[5][:, 0:TI * NE].rearrange("p (i n) -> p i n", i=TI)
                for k in range(NK):
                    TT(prod4[:, TI * k:TI * k + TI, :], oh[:, TI * k:TI * k + TI, :], rk, ALU.mult).then_inc(c.step(), 1)
                e.wait_ge(c.sem, c.last())
                V.tensor_reduce(rank4, prod4, AX, ALU.add).then_inc(c.step(), 1)
                e.wait_ge(c.sem, c.last())
                STT(codes, eidf, float(CAP), rank4, ALU.mult, ALU.add).then_inc(c.step(), 1)
                TS(full4, rank4, float(CAP), NO_SLOT, ALU.is_ge, ALU.mult).then_inc(c.step(), 1)
                e.wait_ge(c.sem, c.last())
                TT(codes, codes, full4, ALU.add).then_inc(c.step(), 1)

                def extra_units():
                    V.tensor_copy(counts, bank[5][:, 2 * NE:3 * NE]).then_inc(c.step(), 1)
                    TS(full4, rank4, float(CAP), NO_SLOT, ALU.is_lt, ALU.mult).then_inc(c.step(), 1)
                    e.wait_ge(c.sem, c.last())
                    TT(over, counts.unsqueeze(2).to_broadcast([P, NE, SEQ // CAP - 1]),
                       thr_cap.unsqueeze(1).to_broadcast([P, NE, SEQ // CAP - 1]), ALU.is_gt).then_inc(c.step(), 1)
                    e.wait_ge(c.sem, c.last())
                    V.tensor_reduce(units, over, AX, ALU.add).then_inc(c.step(), 1)
                    e.wait_ge(c.sem, c.last())
                    V.tensor_tensor_scan(out=upto, data0=ones[:, 0:NE], data1=units, initial=0.0, op0=ALU.mult, op1=ALU.add).then_inc(c.step(), 1)
                    e.wait_ge(c.sem, c.last())
                    TT(units, upto, units, ALU.subtract).then_inc(c.step(), 1)
                    e.wait_ge(c.sem, c.last())
                    TT(prod4, oh, units.unsqueeze(1).to_broadcast([P, NK * TI, NE]), ALU.mult).then_inc(c.step(), 1)
                    TS(fg4, thr_grp[0:1, :], upto[0:1, NE - 1:NE], None, ALU.is_lt).then_inc(c.step(), 1)
                    TT(later, upto[0:1, :].unsqueeze(1).to_broadcast([1, MAXX, NE]),
                       iota[0:1, 0:MAXX].unsqueeze(2).to_broadcast([1, MAXX, NE]), ALU.is_le).then_inc(c.step(), 1)
                    e.wait_ge(c.sem, c.last())
                    V.tensor_reduce(base4, prod4, AX, ALU.add).then_inc(c.step(), 1)
                    V.tensor_reduce(fgrp[0:1, 0:1], fg4, AX, ALU.add).then_inc(c.step(), 1)
                    V.tensor_reduce(xe, later, AX, ALU.add).then_inc(c.step(), 1)
                    e.wait_ge(c.sem, c.last())
                    TS(base4, base4, float(CAP), -float(CAP), ALU.mult, ALU.add).then_inc(c.step(), 1)
                    V.tensor_copy(xinfo[0:1, ds(l, 1), 0:1], fgrp[0:1, 0:1].unsqueeze(1)).then_inc(c.step(), 1)
                    V.tensor_copy(xinfo[0:1, ds(l, 1), 1:2], xsum[0:1, :].unsqueeze(1)).then_inc(c.step(), 1)
                    TS(xinfo[0:1, ds(l, 1), 2:2 + MAXX], xe.unsqueeze(1), float(NE - 1), None, ALU.min).then_inc(c.step(), 1)
                    e.wait_ge(c.sem, c.last())
                    TT(base4, base4, rank4, ALU.add).then_inc(c.step(), 1)
                    TT(xsum[0:1, :], xsum[0:1, :], fgrp[0:1, 0:1], ALU.add).then_inc(routed.sem, 1)
                    e.wait_ge(c.sem, c.last())
                    TT(xcodes, base4, full4, ALU.add).then_inc(c.step(), 1)

                e.wait_ge(c.sem, c.last())
                experts(main, l * GROUPS, OVERLAPPED, codes, extra_units)
                c.end()
                e.wait_ge(c.sem, c.last())
                count, prior = extra_groups(e, l)
                with e.Fori(1, GROUPS) as g:
                    experts(main, l * GROUPS + g, IN_TURN, codes)
                with e.If(count > 0):
                    with e.Fori(0, count) as t:
                        experts(extra, prior + t, IN_TURN, xcodes)
                layer_sums(e, l, count, prior)


INS = ["x", "positions", "norm_mix_g", "w_in", "attn_q_norm_g", "attn_k_norm_g", "lambda_q1", "lambda_k1",
       "lambda_q2", "lambda_k2", "attn_subln_g", "hgrn_lower_bounds", "hgrn_norm_g", "conv_w", "w_out",
       "norm_ffn_g", "router_group_w", "router_group_b", "router_expert_w", "router_expert_b",
       "expert_w_gate", "expert_w_up", "expert_w_down"]


def kernel(**inputs):
    import numpy as _np
    import concourse.bacc as _bacc
    from concourse import mybir as _mybir
    from concourse.bass_utils import run_bass_kernel_spmd as _run

    nc = _bacc.Bacc("TRN2", target_bir_lowering=False, num_devices=1)
    arrays, aps = {}, {}
    for name in INS:
        v = _np.ascontiguousarray(inputs[name])
        arrays[f"in_{name}"] = v
        aps[name] = nc.dram_tensor(f"in_{name}", v.shape, _mybir.dt.from_np(v.dtype), kind="ExternalInput").ap()
    shape = arrays["in_x"].shape
    out = nc.dram_tensor("out", shape, _mybir.dt.float32, kind="ExternalOutput").ap()
    hybrid_trunk(nc, aps, out)
    r = _run(nc, [arrays], core_ids=[0])
    return r.results[0]["out"]
```
